# Optimizing a Trainium2 kernel written in Bass

```python
import math
import jax, jax.numpy as jnp
from jax import lax
import numpy as np

D_MODEL = 1024
BATCH = 1
SEQ = 256
DEPTH = 2

CTX_LEN = 256
GRID_W = 64
HEAD_DIM = 64
SSM_WIDTH = 512
SSM_GROUP = 16
SSM_GROUPS = SSM_WIDTH // SSM_GROUP
SSM_STATE = 64
DT_MIN = 0.001
DT_MAX = 0.1
GQA_HEADS = 8
GQA_KV_HEADS = 2
GQA_WIDTH = GQA_HEADS * HEAD_DIM
GQA_KV_WIDTH = GQA_KV_HEADS * HEAD_DIM
NA_HEADS = 8
NA_WIDTH = NA_HEADS * HEAD_DIM
NA_WIN_H = 8
NA_WIN_W = 16
Q_BLOCK = 128
ROPE_BASE = 10000.0
N_BRANCH = 3
IN_WIDTHS = (SSM_WIDTH, GQA_WIDTH, GQA_KV_WIDTH, GQA_KV_WIDTH, NA_WIDTH, NA_WIDTH, NA_WIDTH, N_BRANCH * D_MODEL)
IN_WIDTH = sum(IN_WIDTHS)
N_EXPERTS = 16
N_EXPERT_GROUPS = 4
EXPERTS_PER_GROUP = N_EXPERTS // N_EXPERT_GROUPS
TOP_K = 2
EXPERT_FF = 512
NORM_EPS = 1e-6

kernel_name = "hybrid_s5_gqa_natten_moe_dit"

def rmsnorm(x, g):
    xf = x.astype(jnp.float32)
    y = xf * lax.rsqrt(jnp.mean(xf * xf, axis=-1, keepdims=True) + NORM_EPS)
    return (y * g.astype(jnp.float32)).astype(x.dtype)

def modulate(h, shift, scale):
    return h * (1.0 + scale) + shift

def axial_rope_tables(n_tokens):
    t = jnp.arange(n_tokens)
    row = (t // GRID_W).astype(jnp.float32)
    col = (t % GRID_W).astype(jnp.float32)
    n_freq = HEAD_DIM // 4
    inv = ROPE_BASE ** (-jnp.arange(n_freq, dtype=jnp.float32) / n_freq)
    ang = jnp.stack([row[:, None] * inv, col[:, None] * inv], axis=1)
    return jnp.cos(ang), jnp.sin(ang)

def apply_axial_rope(x, cos, sin):
    b, s, h, d = x.shape
    xr = x.astype(jnp.float32).reshape(b, s, h, 2, 2, d // 4)
    x1, x2 = xr[..., 0, :], xr[..., 1, :]
    cs, sn = cos[None, :, None], sin[None, :, None]
    out = jnp.stack([x1 * cs - x2 * sn, x2 * cs + x1 * sn], axis=-2)
    return out.reshape(b, s, h, d).astype(x.dtype)

def dense_attend(q, k, v):
    b, lq, hq, d = q.shape
    hk = k.shape[2]
    qg = q.reshape(b, lq, hk, hq // hk, d)
    s = jnp.einsum('bqkgd,bskd->bkgqs', qg, k).astype(jnp.float32) * (d ** -0.5)
    p = jax.nn.softmax(s, axis=-1).astype(v.dtype)
    return jnp.einsum('bkgqs,bskd->bqkgd', p, v).reshape(b, lq, hq * d)

def gqa_latent(q_lat, k_ctx, v_ctx, k_lat, v_lat):
    bsz, n_lat, hq, hd = q_lat.shape
    k_all = jnp.concatenate([k_ctx, k_lat], axis=1)
    v_all = jnp.concatenate([v_ctx, v_lat], axis=1)
    qb = q_lat.reshape(bsz, n_lat // Q_BLOCK, Q_BLOCK, hq, hd).transpose(1, 0, 2, 3, 4)
    out = lax.map(lambda qblk: dense_attend(qblk, k_all, v_all), qb)
    return out.transpose(1, 0, 2, 3).reshape(bsz, n_lat, hq * hd)

def neighborhood_attention(q_lat, k_lat, v_lat, k_ctx, v_ctx, rpb):
    bsz, n_lat, nh, hd = q_lat.shape
    rows = n_lat // GRID_W
    win_h = min(NA_WIN_H, rows)
    scale = hd ** -0.5
    qg = q_lat.reshape(bsz, rows, GRID_W, nh, hd)
    kg = k_lat.reshape(bsz, rows, GRID_W, nh, hd)
    vg = v_lat.reshape(bsz, rows, GRID_W, nh, hd)
    col = jnp.arange(GRID_W)
    col_start = jnp.clip(col - NA_WIN_W // 2, 0, GRID_W - NA_WIN_W)
    col_mask = (col[None, :] >= col_start[:, None]) & (col[None, :] < col_start[:, None] + NA_WIN_W)
    col_off = jnp.clip(col[None, :] - col[:, None], -(NA_WIN_W - 1), NA_WIN_W - 1) + (NA_WIN_W - 1)
    rpb_cols = rpb[:, :, col_off]

    def row_block(args):
        r, q_row = args
        r_start = jnp.clip(r - win_h // 2, 0, rows - win_h)
        kb = lax.dynamic_slice_in_dim(kg, r_start, win_h, axis=1)
        vb = lax.dynamic_slice_in_dim(vg, r_start, win_h, axis=1)
        row_off = r_start + jnp.arange(win_h) - r + (NA_WIN_H - 1)
        bias = rpb_cols[:, row_off].transpose(0, 2, 1, 3)
        s_loc = jnp.einsum('bqhd,bikhd->bhqik', q_row, kb).astype(jnp.float32) * scale + bias[None]
        s_loc = jnp.where(col_mask[None, None, :, None, :], s_loc, -jnp.inf)
        s_loc = s_loc.reshape(bsz, nh, GRID_W, win_h * GRID_W)
        s_ctx = jnp.einsum('bqhd,bchd->bhqc', q_row, k_ctx).astype(jnp.float32) * scale
        p = jax.nn.softmax(jnp.concatenate([s_loc, s_ctx], axis=-1), axis=-1).astype(vb.dtype)
        p_loc = p[..., :win_h * GRID_W].reshape(bsz, nh, GRID_W, win_h, GRID_W)
        p_ctx = p[..., win_h * GRID_W:]
        return (jnp.einsum('bhqik,bikhd->bqhd', p_loc, vb)
                + jnp.einsum('bhqc,bchd->bqhd', p_ctx, v_ctx))

    out = lax.map(row_block, (jnp.arange(rows), qg.transpose(1, 0, 2, 3, 4)))
    return out.transpose(1, 0, 2, 3, 4).reshape(bsz, n_lat, nh * hd)

def _recurrence_combine(left, right):
    a_l, b_l = left
    a_r, b_r = right
    return (a_l * a_r, a_r * b_l + b_r)

def s5_bidirectional(u_ctx, u_lat, lam_re, lam_im, log_dt, b_re, b_im, c_re, c_im, d_skip, need_ctx):
    f32 = jnp.float32
    n_ctx = u_ctx.shape[1]
    n_lat = u_lat.shape[1]

    def scan_direction(seq, d):
        lam = lax.complex(lam_re[d].astype(f32), lam_im[d].astype(f32))
        dt = jnp.exp(log_dt[d].astype(f32))[:, None]
        lam_bar = jnp.exp(lam * dt)
        b_bar = ((lam_bar - 1.0) / lam)[..., None] * lax.complex(b_re[d].astype(f32), b_im[d].astype(f32))
        bsz, length, _ = seq.shape
        ug = seq.astype(f32).reshape(bsz, length, SSM_GROUPS, SSM_GROUP)
        bu = jnp.einsum('blgh,gph->blgp', ug.astype(jnp.complex64), b_bar)
        a = jnp.broadcast_to(lam_bar, (1, length, SSM_GROUPS, SSM_STATE))
        _, states = lax.associative_scan(_recurrence_combine, (a, bu), axis=1)
        return states

    def readout(states, d):
        cm = lax.complex(c_re[d].astype(f32), c_im[d].astype(f32))
        y = jnp.einsum('blgp,ghp->blgh', states, cm).real
        return y.reshape(y.shape[0], y.shape[1], SSM_WIDTH)

    st_f = scan_direction(jnp.concatenate([u_ctx, u_lat], axis=1), 0)
    st_b = jnp.flip(scan_direction(jnp.flip(jnp.concatenate([u_lat, u_ctx], axis=1), axis=1), 1), axis=1)
    dsk = d_skip.astype(f32)
    y_lat = (readout(st_f[:, n_ctx:], 0) + readout(st_b[:, :n_lat], 1)
             + dsk * u_lat.astype(f32)).astype(u_lat.dtype)
    y_ctx = None
    if need_ctx:
        y_ctx = (readout(st_f[:, :n_ctx], 0) + readout(st_b[:, n_lat:], 1)
                 + dsk * u_ctx.astype(f32)).astype(u_ctx.dtype)
    return y_ctx, y_lat

def glu(y, w_glu):
    z = jax.nn.gelu(y)
    return z * jax.nn.sigmoid(z @ w_glu)

def gated_merge(branches, gates, w_branch, w_out):
    b, l, _ = gates.shape
    g = jax.nn.sigmoid(gates.reshape(b, l, N_BRANCH, D_MODEL))
    merged = g[:, :, 0] * (branches[0] @ w_branch[0])
    for i in range(1, N_BRANCH):
        merged = merged + g[:, :, i] * (branches[i] @ w_branch[i])
    return merged @ w_out

def hybrid_mixer(h_ctx, h_lat, cos, sin, w_in, lam_re, lam_im, log_dt, b_re, b_im, c_re, c_im,
                 d_skip, w_glu, q_norm_g, k_norm_g, rpb, w_branch, w_out, need_ctx):
    bsz, n_ctx, _ = h_ctx.shape
    proj = jnp.concatenate([h_ctx, h_lat], axis=1) @ w_in
    splits = [int(v) for v in np.cumsum(IN_WIDTHS)[:-1]]
    u, qa, ka, va, qn, kn, vn, gates = jnp.split(proj, splits, axis=-1)
    cpart = lambda t: t[:, :n_ctx]
    lpart = lambda t: t[:, n_ctx:]
    heads = lambda t, n: t.reshape(t.shape[0], t.shape[1], n, HEAD_DIM)

    ssm_ctx, ssm_lat = s5_bidirectional(cpart(u), lpart(u), lam_re, lam_im, log_dt, b_re, b_im,
                                        c_re, c_im, d_skip, need_ctx)
    qa_h = rmsnorm(heads(qa, GQA_HEADS), q_norm_g)
    ka_h = rmsnorm(heads(ka, GQA_KV_HEADS), k_norm_g)
    va_h = heads(va, GQA_KV_HEADS)
    gqa_lat = gqa_latent(apply_axial_rope(lpart(qa_h), cos, sin), cpart(ka_h), cpart(va_h),
                         apply_axial_rope(lpart(ka_h), cos, sin), lpart(va_h))
    qn_h, kn_h, vn_h = heads(qn, NA_HEADS), heads(kn, NA_HEADS), heads(vn, NA_HEADS)
    na_lat = neighborhood_attention(lpart(qn_h), lpart(kn_h), lpart(vn_h), cpart(kn_h), cpart(vn_h), rpb)

    y_lat = gated_merge([glu(ssm_lat, w_glu), gqa_lat, na_lat], lpart(gates), w_branch, w_out)
    y_ctx = None
    if need_ctx:
        gqa_ctx = dense_attend(cpart(qa_h), cpart(ka_h), cpart(va_h))
        na_ctx = dense_attend(cpart(qn_h), cpart(kn_h), cpart(vn_h))
        y_ctx = gated_merge([glu(ssm_ctx, w_glu), gqa_ctx, na_ctx], cpart(gates), w_branch, w_out)
    return y_ctx, y_lat

def moe_ffn(h, router_w, router_b, w_gate, w_up, w_down):
    probs = jax.nn.softmax((h @ router_w).astype(jnp.float32), axis=-1)
    sel = probs + router_b.astype(jnp.float32)
    grp = sel.reshape(-1, N_EXPERT_GROUPS, EXPERTS_PER_GROUP)
    grp_score = jnp.sum(lax.top_k(grp, TOP_K)[0], axis=-1)
    best = jnp.argmax(grp_score, axis=-1)
    in_grp = (jnp.arange(N_EXPERTS) // EXPERTS_PER_GROUP)[None, :] == best[:, None]
    _, idx = lax.top_k(jnp.where(in_grp, sel, -jnp.inf), TOP_K)
    w_sel = jnp.take_along_axis(probs, idx, axis=-1)
    w_sel = w_sel / jnp.sum(w_sel, axis=-1, keepdims=True)
    combine = jnp.sum(jax.nn.one_hot(idx, N_EXPERTS, dtype=jnp.float32) * w_sel[..., None], axis=1)
    combine = combine.astype(h.dtype)
    out = jnp.zeros_like(h)
    for e in range(N_EXPERTS):
        y_e = (jax.nn.silu(h @ w_gate[e]) * (h @ w_up[e])) @ w_down[e]
        out = out + combine[:, e:e + 1] * y_e
    return out

def setup_inputs(seed: int = 0) -> dict:
    key = jax.random.key(seed)
    ks = jax.random.split(key, 32)
    f32 = jnp.float32
    nrm = lambda k, shape, scale: jax.random.normal(k, shape, f32) * scale
    lam_shape = (DEPTH, 2, SSM_GROUPS, SSM_STATE)
    n_idx = jnp.arange(SSM_STATE, dtype=f32)
    return {
        "x": nrm(ks[0], (BATCH, SEQ, D_MODEL), 1.0),
        "c": nrm(ks[1], (BATCH, D_MODEL), 1.0),
        "ctx": nrm(ks[2], (BATCH, CTX_LEN, D_MODEL), 1.0),
        "c_ctx": nrm(ks[3], (D_MODEL,), 1.0),
        "w_mod": nrm(ks[4], (DEPTH, D_MODEL, 6 * D_MODEL), 0.5 * D_MODEL ** -0.5),
        "b_mod": nrm(ks[5], (DEPTH, 6 * D_MODEL), 0.02),
        "norm1_g": 1.0 + nrm(ks[6], (DEPTH, D_MODEL), 0.02),
        "norm2_g": 1.0 + nrm(ks[7], (DEPTH, D_MODEL), 0.02),
        "w_in": nrm(ks[8], (DEPTH, D_MODEL, IN_WIDTH), D_MODEL ** -0.5),
        "ssm_lam_re": -0.5 * jnp.exp(nrm(ks[9], lam_shape, 0.05)),
        "ssm_lam_im": math.pi * n_idx + nrm(ks[10], lam_shape, 0.01),
        "ssm_log_dt": jax.random.uniform(ks[11], (DEPTH, 2, SSM_GROUPS), f32, math.log(DT_MIN), math.log(DT_MAX)),
        "ssm_b_re": nrm(ks[12], (DEPTH, 2, SSM_GROUPS, SSM_STATE, SSM_GROUP), (2 * SSM_GROUP) ** -0.5),
        "ssm_b_im": nrm(ks[13], (DEPTH, 2, SSM_GROUPS, SSM_STATE, SSM_GROUP), (2 * SSM_GROUP) ** -0.5),
        "ssm_c_re": nrm(ks[14], (DEPTH, 2, SSM_GROUPS, SSM_GROUP, SSM_STATE), SSM_STATE ** -0.5),
        "ssm_c_im": nrm(ks[15], (DEPTH, 2, SSM_GROUPS, SSM_GROUP, SSM_STATE), SSM_STATE ** -0.5),
        "ssm_d": nrm(ks[16], (DEPTH, SSM_WIDTH), 1.0),
        "ssm_w_glu": nrm(ks[17], (DEPTH, SSM_WIDTH, SSM_WIDTH), SSM_WIDTH ** -0.5),
        "gqa_q_norm_g": 1.0 + nrm(ks[18], (DEPTH, HEAD_DIM), 0.02),
        "gqa_k_norm_g": 1.0 + nrm(ks[19], (DEPTH, HEAD_DIM), 0.02),
        "na_rpb": nrm(ks[20], (DEPTH, NA_HEADS, 2 * NA_WIN_H - 1, 2 * NA_WIN_W - 1), 0.1),
        "w_branch": nrm(ks[21], (DEPTH, N_BRANCH, SSM_WIDTH, D_MODEL), SSM_WIDTH ** -0.5),
        "w_out": nrm(ks[22], (DEPTH, D_MODEL, D_MODEL), D_MODEL ** -0.5),
        "router_w": nrm(ks[23], (D_MODEL, N_EXPERTS), D_MODEL ** -0.5),
        "router_b": nrm(ks[24], (N_EXPERTS,), 0.01),
        "moe_w_gate": nrm(ks[25], (DEPTH, N_EXPERTS, D_MODEL, EXPERT_FF), D_MODEL ** -0.5),
        "moe_w_up": nrm(ks[26], (DEPTH, N_EXPERTS, D_MODEL, EXPERT_FF), D_MODEL ** -0.5),
        "moe_w_down": nrm(ks[27], (DEPTH, N_EXPERTS, EXPERT_FF, D_MODEL), EXPERT_FF ** -0.5),
        "final_norm_g": 1.0 + nrm(ks[28], (D_MODEL,), 0.02),
    }

def reference(x, c, ctx, c_ctx, w_mod, b_mod, norm1_g, norm2_g, w_in,
              ssm_lam_re, ssm_lam_im, ssm_log_dt, ssm_b_re, ssm_b_im, ssm_c_re, ssm_c_im,
              ssm_d, ssm_w_glu, gqa_q_norm_g, gqa_k_norm_g, na_rpb, w_branch, w_out,
              router_w, router_b, moe_w_gate, moe_w_up, moe_w_down, final_norm_g):
    bsz, n_lat, d_model = x.shape
    n_ctx = ctx.shape[1]
    cos, sin = axial_rope_tables(n_lat)
    cond_lat = jax.nn.silu(c)
    cond_ctx = jax.nn.silu(c_ctx)
    for layer in range(DEPTH):
        need_ctx = layer < DEPTH - 1
        sh1, sc1, g1, sh2, sc2, g2 = jnp.split((cond_lat @ w_mod[layer] + b_mod[layer])[:, None, :], 6, axis=-1)
        csh1, csc1, cg1, csh2, csc2, cg2 = jnp.split(cond_ctx @ w_mod[layer] + b_mod[layer], 6, axis=-1)
        h_lat = modulate(rmsnorm(x, norm1_g[layer]), sh1, sc1)
        h_ctx = modulate(rmsnorm(ctx, norm1_g[layer]), csh1, csc1)
        y_ctx, y_lat = hybrid_mixer(h_ctx, h_lat, cos, sin, w_in[layer],
                                    ssm_lam_re[layer], ssm_lam_im[layer], ssm_log_dt[layer],
                                    ssm_b_re[layer], ssm_b_im[layer], ssm_c_re[layer], ssm_c_im[layer],
                                    ssm_d[layer], ssm_w_glu[layer], gqa_q_norm_g[layer], gqa_k_norm_g[layer],
                                    na_rpb[layer], w_branch[layer], w_out[layer], need_ctx)
        x = x + g1 * y_lat
        h_lat = modulate(rmsnorm(x, norm2_g[layer]), sh2, sc2).reshape(-1, d_model)
        if need_ctx:
            ctx = ctx + cg1 * y_ctx
            h_ctx = modulate(rmsnorm(ctx, norm2_g[layer]), csh2, csc2).reshape(-1, d_model)
            y = moe_ffn(jnp.concatenate([h_ctx, h_lat], axis=0), router_w, router_b,
                        moe_w_gate[layer], moe_w_up[layer], moe_w_down[layer])
            ctx = ctx + cg2 * y[:bsz * n_ctx].reshape(ctx.shape)
            y = y[bsz * n_ctx:]
        else:
            y = moe_ffn(h_lat, router_w, router_b, moe_w_gate[layer], moe_w_up[layer], moe_w_down[layer])
        x = x + g2 * y.reshape(x.shape)
    return rmsnorm(x, final_norm_g)


_drawn_inputs = setup_inputs


def setup_inputs(seed=0):
    import zlib

    import numpy as np

    out = dict(_drawn_inputs(seed))
    spreads = {}
    factors = {'norm1_g': 3.923,
     'ssm_lam_re': 8.0,
     'ssm_b_re': 2.842,
     'ssm_c_im': 4.961,
     'gqa_q_norm_g': 8.0,
     'gqa_k_norm_g': 8.0,
     'na_rpb': 8.0,
     'final_norm_g': 2.735}
    for name, (base, spread) in spreads.items():
        noise = np.random.default_rng([zlib.crc32(name.encode()), seed]).standard_normal(out[name].shape)
        drawn = base * np.exp(spread * noise) if base else spread * noise
        out[name] = __import__('jax').numpy.asarray(drawn.astype(out[name].dtype))
    for name, factor in factors.items():
        out[name] = (out[name] * factor).astype(out[name].dtype)
    return out
```

```python
import math
from contextlib import ExitStack

import numpy as np

import concourse.bass as bass
from concourse import mybir

F32 = mybir.dt.float32
ALU = mybir.AluOpType
ACT = mybir.ActivationFunctionType
AX = mybir.AxisListType

P = 128
D = 1024
KD = D // P
CTX, LAT = 256, 256
NTOK = CTX + LAT
LAYERS = 2
GRID_W = 64
GRID_H = LAT // GRID_W
HD = 64
HEADS = 8
WID = 512
KW = WID // P
WIN_W = 16
RPB_ROWS, RPB_COLS = 15, 31
RPB_PAD = 2 * GRID_W - 1
NGRP, GRP, NST = 32, 16, 64
STEP = P // GRP
NCH = NTOK // STEP
NCC = CTX // STEP
GQ = 4
NQ = NGRP // GQ
NPOS = 2 * STEP + 1
NEXP, EGRP = 16, 4
KF = 4
EPS = 1e-6
FAR = 1e30
ROUND = 12582912.0

SLOT = 2048
RING = 6
S_MOD, S_U, S_QA, S_KV, S_QN, S_KN, S_VN, S_GLU, S_MIX, S_OUT, S_MOE = (
    0, 24, 26, 28, 29, 31, 33, 35, 36, 54, 58)
PER_EXPERT = 6
PER_LAYER = S_MOE + NEXP * PER_EXPERT
NSLOT = LAYERS * PER_LAYER



def columns(*sizes):
    at, out = 0, {}
    for name, n in sizes:
        out[name] = slice(at, at + n)
        at += n
    return out, at


MISC, N_MISC = columns(("bmod", 48), ("n1", KD), ("n2", KD), ("qg", 1), ("kg", 1))
SSM, N_SSM = columns(("lre", NGRP), ("lim", NGRP), ("ldt", NGRP), ("bre", NGRP * GRP), ("bim", NGRP * GRP),
                     ("cre", NGRP * GRP), ("cim", NGRP * GRP))
CON, N_CON = columns(("ident", P), ("head_mean", P), ("model_mean", P), ("rot", P), ("cos", LAT), ("sin", LAT),
                     ("iota", NEXP), ("far_cols", GRID_W), ("rw", KD * NEXP), ("rb", NEXP), ("fg", KD),
                     ("c", 2 * KD))

TWO_PI_1 = 6.28125
TWO_PI_2 = float(np.float32(2 * math.pi - TWO_PI_1))
TWO_PI_3 = 2 * math.pi - TWO_PI_1 - TWO_PI_2
PI_BELOW = 3.1415925

COMB = 23
BANKS = 4
MOE_JOBS = 2 * KF + KD


def attention_units(layer):
    return [(br, i, half, q0, CTX if q0 < CTX else NTOK)
            for br in range(2) for i in range(KW) for half in range(2)
            for q0 in range(0 if layer == 0 else CTX, NTOK, P)]


def tile_jobs():
    names = []
    for l in range(LAYERS):
        names += [(l, "mod"), (l, "ms1")]
        names += [(l, "u", m) for m in range(KW)]
        for q in range(NQ):
            names += [(l, "wt", q, 0), (l, "wt", q, 1), (l, "st", q)]
        names += [(l, "qa", m) for m in range(KW)] + [(l, "ka"), (l, "va")]
        names += [(l, "qn", m) for m in range(KW)] + [(l, "kn", m) for m in range(KW)]
        names += [(l, "vn", m) for m in range(KW)]
        for m in range(KW + 1):
            names += [(l, "qk_ms", m), (l, "rope", m)]
        for q in range(NQ + 1):
            names += [(l, "z", q, 0), (l, "z", q, 1)] if q < NQ else []
            names += [(l, "y", q - 1)] if q else []
        names += [(l, "sc", u) for u in range(len(attention_units(l)))]
        names += [(l, "glu", m) for m in range(KW)]
        for hf in range(2):
            for b in range(3):
                for m in range(KW):
                    names += [(l, "gate", hf, b, m), (l, "br", hf, b, m)]
        names += [(l, "wo", m) for m in range(KD)]
        names += [(l, "ms2"), (l, "rt")]
        names += [(l, "comb", e) for e in range(NEXP)]
        names += [(l, "moe", n) for n in range(NEXP * MOE_JOBS)]
    names.append((LAYERS, "ms"))
    return {n: i for i, n in enumerate(names)}


JOB = tile_jobs()


class Link:

    def __init__(self, eng, sem):
        self.eng, self.sem, self.n = eng, sem, 0

    def __call__(self, ins, more=0):
        self.n += 1
        ins.then_inc(self.sem, 1)
        self.eng.wait_ge(self.sem, self.n + more)


def spread(ap, axis, n):
    v = ap.unsqueeze(axis)
    shape = list(v.shape)
    shape[axis] = n
    return v.broadcast_to(shape)


def backbone(nc, xT, wpack, misc, ssm, dskip, rpb, const, outT):
    ctx = ExitStack()
    with ctx:
        def sb(name, shape):
            return ctx.enter_context(nc.sbuf_tensor(name, shape, F32))

        def sem(name):
            return ctx.enter_context(nc.semaphore(name))

        def sems(name, n):
            return [sem(f"{name}{i}") for i in range(n)]

        u_dram = nc.dram_tensor("u_scratch", [WID, STEP, NCH], F32, kind="Internal").ap()
        y_dram = nc.dram_tensor("y_scratch", [WID, STEP, NCH], F32, kind="Internal").ap()

        x = sb("x", [P, KD, NTOK])
        h = sb("h", [P, KD, NTOK])
        ring = sb("ring", [P, RING, SLOT])
        con = sb("con", [P, N_CON])
        mis = sb("mis", [P, LAYERS, N_MISC])
        qa = sb("qa", [P, KW, NTOK])
        ka = sb("ka", [P, NTOK])
        va = sb("va", [P, NTOK // P, P])
        qn = sb("qn", [P, KW, NTOK])
        kn = sb("kn", [P, KW, NTOK])
        vn = sb("vn", [P, NTOK // P, WID])
        mod = sb("mod", [P, 6, KD, 2])
        amul = sb("amul", [P, 2, KD, 2])
        csil = sb("csil", [P, KD, 2])
        rstd = sb("rstd", [P, NTOK])
        qsq = sb("qsq", [P, NTOK])
        qrs = rstd
        qrt = sb("qrt", [P, LAT])
        qg8 = sb("qg8", [P, 1])
        smx = sb("smx", [P, 3, 64])
        ARENA = 20224
        arena = sb("arena", [P, ARENA])

        def cut(start, shape, parts=P):
            n = int(np.prod(shape))
            assert start + n <= ARENA, (start, shape)
            v = arena[0:parts, start:start + n]
            if len(shape) > 1:
                names = "abcd"[:len(shape)]
                v = v.rearrange(f"p ({' '.join(names)}) -> p {' '.join(names)}", **dict(zip(names, shape)))
            return v, start + n

        a0 = 0
        sm, a0 = cut(a0, [N_SSM])
        ug, a0 = cut(a0, [NGRP, NCH])
        st, a0 = cut(a0, [2, NGRP, NCH + 1])
        bb, a0 = cut(a0, [2, NGRP, GRP])
        pw, a0 = cut(a0, [2, STEP + 1, NGRP])
        pww, a0 = cut(a0, [2, STEP, NGRP])
        pws, a0 = cut(a0, [2, NPOS, NGRP])
        t8, a0 = cut(a0, [12, NGRP])
        sst, a0 = cut(a0, [2, 2, NGRP])
        a8s, a0 = cut(a0, [2, 2, NGRP])
        up, a1 = cut(a0, [KW, STEP * NCH])
        wm, a1 = cut(a1, [2, GQ, STEP, GRP])
        wt, a1 = cut(a1, [2, GQ, P])
        wtmp, a1 = cut(a1, [GQ, STEP, GRP])
        cp, a2 = cut(a0, [2, 2 * GQ, NPOS, GRP])
        ctmp, a2 = cut(a2, [GQ, NPOS, GRP])
        zs, a2 = cut(a2, [GQ, (NPOS - 2) * GRP], parts=GRP)
        tm, a2 = cut(a2, [2, GQ, P])
        dsk, a2 = cut(a2, [NGRP, GRP], parts=GRP)
        a3 = 0
        bo = [None] * 3
        for b in range(3):
            bo[b], a3 = cut(a3, [KW, NTOK])
        bias, a4 = cut(a3, [2, HEADS, GRID_H, GRID_W])
        probs, a5 = cut(a4, [3, NTOK])
        pt, a5 = cut(a5, [2, NTOK // P, P])
        yt, a5 = cut(a5, [KW, STEP * NCH])
        z, a5 = cut(a5, [KW, NTOK])
        mg, _ = cut(a3, [KD, NTOK])
        sig, a6 = cut(a4, [2, NTOK])
        prod, a6 = cut(a6, [2, NTOK])
        comb_bc, a7 = cut(0, [NEXP, NTOK])
        hid, a7 = cut(a7, [KF, NTOK])
        act_g, a7 = cut(a7, [2, NTOK])
        act_u, a7 = cut(a7, [2, NTOK])
        rt, a7 = cut(a7, [24, NTOK // P, NEXP])

        tile_ps = ctx.enter_context(nc.psum_tensor("tile_ps", [P, BANKS, 512], F32))
        turn_ps = ctx.enter_context(nc.psum_tensor("turn_ps", [P, 2, 512], F32))
        out_ps = ctx.enter_context(nc.psum_tensor("out_ps", [P, 2, 512], F32))

        const_in = sem("const_in")
        slot_in = sems("slot_in", RING)
        slot_used = sem("slot_used")
        tile_full, tile_free = sems("tile_full", BANKS), sems("tile_free", BANKS)
        turn_full, turn_free = sems("turn_full", 2), sems("turn_free", 2)
        out_full, out_free = sems("out_full", 2), sems("out_free", 2)
        dve_link, act_link, pool_link = sem("dve_link"), sem("act_link"), sem("pool_link")
        csil_done, mod_done = sem("csil_done"), sem("mod_done")
        sq_done, root_done, hx_done, h_done = sem("sq_done"), sem("root_done"), sem("hx_done"), sem("h_done")
        ssm_in = sem("ssm_in")
        u_out, ug_in, y_out, y_in = sem("u_out"), sem("ug_in"), sem("y_out"), sem("y_in")
        wm_done, scan_done = sem("wm_done"), sem("scan_done")
        trig_in, trig_out = sem("trig_in"), sem("trig_out")
        pow_done, cp_done, zd_done, tm_in = sem("pow_done"), sem("cp_done"), sem("zd_done"), sem("tm_in")
        qsq_done, qroot_done, qnorm_done, rope_done = (
            sem("qsq_done"), sem("qroot_done"), sem("qnorm_done"), sem("rope_done"))
        bias_in, bias_done = sem("bias_in"), sem("bias_done")
        max_done, inv_done, prob_done = sem("max_done"), sem("inv_done"), sem("prob_done")
        gelu_done, glu_done, mix_done = sem("gelu_done"), sem("glu_done"), sem("mix_done")
        rl_done, re_done, comb_done, hid_done = sem("rl_done"), sem("re_done"), sem("comb_done"), sem("hid_done")
        fin_done, stored = sem("fin_done"), sem("stored")

        def c(name):
            return con[:, CON[name]]

        def s_(name):
            return sm[:, SSM[name]]

        def bank(job):
            return tile_ps[:, JOB[job] % BANKS, :]

        def wait_full(eng, job, beyond=0):
            n = JOB[job]
            eng.wait_ge(tile_full[n % BANKS], n // BANKS + 1 + beyond)

        def wait_taken(eng, job, beyond=0):
            n = JOB[job]
            eng.wait_ge(tile_free[n % BANKS], n // BANKS + 1 + beyond)

        def wait_bank(pe, job, beyond=0):
            n = JOB[job]
            if n >= BANKS:
                pe.wait_ge(tile_free[n % BANKS], n // BANKS + beyond)

        def full(job, ins):
            ins.then_inc(tile_full[JOB[job] % BANKS], 1)

        def free(job, ins):
            ins.then_inc(tile_free[JOB[job] % BANKS], 1)

        const_dram = const
        units = [attention_units(l) for l in range(LAYERS)]
        n_before = [0, len(units[0])]
        n_lat = [sum(u[0] == 1 and u[3] >= CTX for u in us) for us in units]
        LOADS = 4
        block = ctx.enter_context(nc.Block())

        @block.sync
        def _(sp):
            sp.dma_start(con[:], const_dram).then_inc(const_in, 16)
            sp.dma_start(mis[:], misc.rearrange("l p n -> p l n")).then_inc(const_in, 16)
            sp.dma_start(x[:], xT.rearrange("(k p) n -> p k n", p=P)).then_inc(const_in, 16)
            for n in range(RING):
                sp.dma_start(ring[:, n, :], wpack[n]).then_inc(slot_in[n], 16)
            turns = NSLOT // RING
            with sp.Fori(1, turns) as i:
                for n in range(RING):
                    sp.wait_ge(slot_used, (i - 1) * RING + n + 1)
                    sp.dma_start(ring[:, n, :], wpack[bass.ds(i * RING + n, 1)].rearrange("a p n -> (a p) n"))\
                        .then_inc(slot_in[n], 16)
            for n in range(turns * RING, NSLOT):
                sp.wait_ge(slot_used, n - RING + 1)
                sp.dma_start(ring[:, n % RING, :], wpack[n]).then_inc(slot_in[n % RING], 16)
            for m in range(KD):
                sp.wait_ge(fin_done, m + 1)
                sp.dma_start(outT[m * P:(m + 1) * P, :], h[:, m, CTX:]).then_inc(stored, 16)
            sp.wait_ge(stored, 16 * KD)

        @block.tensor
        def _(pe):
            def mm(out, lhsT, rhs, start=True, stop=True):
                return nc.tensor.matmul(out, lhsT, rhs, start=start, stop=stop)

            def slot(l, n, parts=KD):
                g = l * PER_LAYER + n
                pe.wait_ge(slot_in[g % RING], 16 * (g // RING + 1))
                return ring[:, g % RING, :].rearrange("p (k n) -> p k n", k=parts)

            def product(job, terms, out=None, release=0, begin=True, end=True):
                if begin:
                    wait_bank(pe, job)
                out = bank(job) if out is None else out
                for k, (lhsT, rhs) in enumerate(terms):
                    ins = mm(out, lhsT, rhs, k == 0, k == len(terms) - 1)
                    if k == 0 and release:
                        ins.then_inc(slot_used, release)
                if end:
                    full(job, ins)

            def mean_square(job, nn, c0):
                wait_bank(pe, job)
                for k in range(KD):
                    pe.wait_ge(sq_done, nn * KD + k + 1)
                    ins = mm(bank(job)[:, c0:], c("model_mean"), h[:, k, c0:], k == 0, k == KD - 1)
                full(job, ins)

            def project(job, w, m, src, c0, release=0):
                product(job, [(w[:, k, m * P:(m + 1) * P], src[:, k, c0:]) for k in range(w.shape[1])],
                        bank(job)[:, c0:], release)

            for l in range(LAYERS):
                c0 = 0 if l == 0 else CTX
                if l == 0:
                    pe.wait_ge(const_in, 48)
                    pe.wait_ge(csil_done, 1)
                job = (l, "mod")
                for n in range(24):
                    w = slot(l, S_MOD + n)
                    for t in range(2):
                        col = 4 * n + 2 * t
                        product(job, [(w[:, k, t * P:(t + 1) * P], csil[:, k, :]) for k in range(KD)],
                                bank(job)[:, col:col + 2], int(t == 0 and l + n > 0), col == 0, n == 23 and t == 1)
                mean_square((l, "ms1"), 2 * l, 0)

                pe.wait_ge(h_done, (2 * l + 1) * KD)
                for m in range(KW):
                    project((l, "u", m), slot(l, S_U + m // 2), m % 2, h, 0, 1 - m % 2)
                for q in range(NQ):
                    pe.wait_ge(wm_done, l * NQ + q + 1)
                    for r in range(2):
                        job = (l, "wt", q, r)
                        wait_bank(pe, job)
                        for g in range(GQ):
                            ins = nc.tensor.transpose(bank(job)[:, g * P:(g + 1) * P],
                                                      wm[:, r, g].rearrange("p j h -> p (j h)"), c("ident"))
                        full(job, ins)
                    job = (l, "st", q)
                    wait_bank(pe, job)
                    for r in range(2):
                        wait_taken(pe, (l, "wt", q, r))
                    pe.wait_ge(ug_in, 16 * STEP * (l + 1))
                    for g in range(GQ):
                        for r in range(2):
                            ins = mm(bank(job)[:, (2 * g + r) * NCH:(2 * g + r + 1) * NCH], wt[:, r, g, :],
                                     ug[:, q * GQ + g, :])
                    full(job, ins)
                for m in range(KW):
                    project((l, "qa", m), slot(l, S_QA + m // 2), m % 2, h, c0, 1 - m % 2)
                w = slot(l, S_KV)
                project((l, "ka"), w, 0, h, 0, 1)
                job = (l, "va")
                for t in range(NTOK // P):
                    product(job, [(h[:, k, t * P:(t + 1) * P], w[:, k, P:]) for k in range(KD)],
                            bank(job)[:, t * P:(t + 1) * P], 0, t == 0, t == NTOK // P - 1)
                for m in range(KW):
                    project((l, "qn", m), slot(l, S_QN + m // 2), m % 2, h, c0, 1 - m % 2)
                for m in range(KW):
                    project((l, "kn", m), slot(l, S_KN + m // 2), m % 2, h, 0, 1 - m % 2)
                ws = slot(l, S_VN), slot(l, S_VN + 1)
                for t in range(NTOK // P):
                    job = (l, "vn", t)
                    for n, w in enumerate(ws):
                        product(job, [(h[:, k, t * P:(t + 1) * P], w[:, k, :]) for k in range(KD)],
                                bank(job)[:, n * 256:(n + 1) * 256], int(t + n == 0), n == 0, n == 1)
                for m in range(KW + 1):
                    t = c0 if m < KW else 0
                    pe.wait_ge(qsq_done, l * (KW + 1) + m + 1)
                    product((l, "qk_ms", m), [(c("head_mean"), qsq[:, t:])], bank((l, "qk_ms", m))[:, t:])
                    pe.wait_ge(qnorm_done, l * (KW + 1) + m + 1)
                    v = qa[:, m, CTX:] if m < KW else ka[:, CTX:]
                    product((l, "rope", m), [(c("rot"), v)], bank((l, "rope", m))[:, 0:LAT])
                zw = (NPOS - 2) * GRP
                for q in range(NQ + 1):
                    if q < NQ:
                        pe.wait_ge(cp_done, l * NQ + q + 1)
                        for n in range(2):
                            for g in range(2):
                                gg = 2 * n + g
                                product((l, "z", q, n),
                                        [(bb[:, r, q * GQ + gg, :],
                                          cp[:, r, (q % 2) * GQ + gg, 1:NPOS - 1, :].rearrange("p a b -> p (a b)"))
                                         for r in range(2)],
                                        bank((l, "z", q, n))[0:GRP, g * zw:(g + 1) * zw], 0, g == 0, g == 1)
                    if q:
                        o = q - 1
                        job = (l, "y", o)
                        pe.wait_ge(tm_in, 16 * STEP * (l * NQ + o + 1))
                        pe.wait_ge(scan_done, l + 1)
                        for g in range(GQ):
                            G = o * GQ + g
                            terms = [(tm[:, o % 2, g, :], ug[:, G, :])]
                            for r in range(2):
                                co = cp[:, r, (o % 2) * GQ + g].rearrange("p a b -> p (a b)")
                                terms.append((co[:, (STEP + 1) * GRP:], st[:, r, G, 0:NCH]))
                                s = st[:, r, G, 0:NCH].rearrange("p (a c) -> p a c", a=2)[:, :, ::-1]
                                terms.append((co[:, 0:STEP * GRP], s))
                            product(job, terms, bank(job)[:, g * NCH:(g + 1) * NCH], 0, g == 0, g == GQ - 1)
                us = units[l]
                pe.wait_ge(rope_done, (l + 1) * (KW + 1))
                for t in range(NTOK // P):
                    wait_taken(pe, (l, "vn", t))
                for n in range(len(us) + 3):
                    if n < len(us):
                        br, i, half, q0, nk = us[n]
                        qq, kk = (qa[:, i], ka[:, :]) if br == 0 else (qn[:, i], kn[:, i])
                        a = half * HD
                        product((l, "sc", n), [(qq[a:a + HD, q0:q0 + P], kk[a:a + HD, 0:nk])],
                                bank((l, "sc", n))[:, 0:nk])
                    if 2 <= n < len(us) + 2:
                        N, nk = n_before[l] + n - 2, us[n - 2][4]
                        if N >= 2:
                            pe.wait_ge(turn_free[N % 2], N // 2)
                        pe.wait_ge(prob_done, N + 1)
                        for t in range(nk // P):
                            ins = nc.tensor.transpose(turn_ps[:, N % 2, t * P:(t + 1) * P],
                                                      probs[:, N % 3, t * P:(t + 1) * P], c("ident"))
                        ins.then_inc(turn_full[N % 2], 1)
                    if n >= 3:
                        N, (br, i, half, q0, nk) = n_before[l] + n - 3, us[n - 3]
                        O = (l * 2 + br) * KW + i
                        if (half, q0) == (0, c0) and O >= 2:
                            pe.wait_ge(out_free[O % 2], O // 2)
                        pe.wait_ge(turn_free[N % 2], N // 2 + 1)
                        a = half * HD
                        for t in range(nk // P):
                            v = va[:, t, a:a + HD] if br == 0 else vn[:, t, i * P + a:i * P + a + HD]
                            ins = mm(out_ps[a:a + HD, O % 2, q0:q0 + P], v, pt[:, N % 2, t, :],
                                     t == 0, t == nk // P - 1)
                        if (half, q0) == (1, NTOK - P):
                            ins.then_inc(out_full[O % 2], 1)
                pe.wait_ge(gelu_done, (l + 1) * KW)
                for m in range(KW):
                    project((l, "glu", m), slot(l, S_GLU, KW), m, z, c0, 2 if m == 0 else 0)
                for hf in range(2):
                    for b in range(3):
                        n = S_MIX + (hf * 3 + b) * 3
                        for m in range(KW):
                            w = slot(l, n + (0 if m < 2 else 2))
                            first = hf + b == 0
                            project((l, "gate", hf, b, m), w, m % 2, h, c0,
                                    {0: 1 if first else 2, 2: 1}.get(m, 0))
                            if hf + m == 0:
                                if b == 0:
                                    pe.wait_ge(glu_done, (l + 1) * KW)
                                else:
                                    for O in ((l * 2 + b) * KW - 2, (l * 2 + b) * KW - 1):
                                        pe.wait_ge(out_free[O % 2], O // 2 + 1)
                            project((l, "br", hf, b, m), slot(l, n + 1, KW), m, bo[b], c0)
                pe.wait_ge(mix_done, (l + 1) * 4 * KW)
                for m in range(KD):
                    project((l, "wo", m), slot(l, S_OUT + m // 2), m % 2, mg, c0,
                            {0: 2, 2: 1, 4: 1, 6: 1}.get(m, 0))
                mean_square((l, "ms2"), 2 * l + 1, c0)
                pe.wait_ge(h_done, (2 * l + 2) * KD)
                job = (l, "rt")
                tiles = range(c0 // P, NTOK // P)
                for t in tiles:
                    product(job, [(h[:, k, t * P:(t + 1) * P], c("rw")[:, k * NEXP:(k + 1) * NEXP]) for k in range(KD)],
                            bank(job)[:, t * NEXP:(t + 1) * NEXP], 0, t == tiles[0], t == tiles[-1])
                pe.wait_ge(comb_done, l + 1)
                for e in range(NEXP):
                    job = (l, "comb", e)
                    for t in tiles:
                        product(job, [(rt[:, COMB, t, e:e + 1].broadcast_to([P, P]), c("ident"))],
                                bank(job)[:, t * P:(t + 1) * P], 0, t == tiles[0], t == tiles[-1])
                with pe.Fori(0, NEXP) as i:
                    def expert_slot(k, parts):
                        g = l * PER_LAYER + S_MOE + k
                        pe.wait_ge(slot_in[g % RING], i * 16 + 16 * (g // RING + 1))
                        return ring[:, g % RING, :].rearrange("p (k n) -> p k n", k=parts)

                    def expert_product(k, w, m, src, release):
                        job = (l, "moe", k)
                        wait_bank(pe, job, i * (MOE_JOBS // BANKS))
                        for kk in range(w.shape[1]):
                            ins = mm(bank(job)[:, c0:], w[:, kk, m * P:(m + 1) * P], src[:, kk, c0:],
                                     kk == 0, kk == w.shape[1] - 1)
                            if kk == 0 and release:
                                ins.then_inc(slot_used, release)
                        full(job, ins)

                    for f in range(KF):
                        wg = expert_slot(2 * (f // 2), KD)
                        expert_product(2 * f, wg, f % 2, h, {0: 1, 2: 2}.get(f, 0))
                        wu = expert_slot(2 * (f // 2) + 1, KD)
                        expert_product(2 * f + 1, wu, f % 2, h, 0)
                    pe.wait_ge(hid_done, i * KF + (l * NEXP + 1) * KF)
                    for m in range(KD):
                        wd = expert_slot(4 + m // 4, KF)
                        expert_product(2 * KF + m, wd, m % 4, hid, {0: 2, 4: 1}.get(m, 0))
            mean_square((LAYERS, "ms"), 2 * LAYERS, CTX)

        @block.scalar
        def _(act):
            A = nc.scalar.activation
            link = Link(act, act_link)

            def copy(job, out, src):
                wait_full(act, job)
                free(job, nc.scalar.copy(out, src))

            def squares(nn, c0, ready):
                for k in range(KD):
                    ready(k)
                    A(h[:, k, c0:], x[:, k, c0:], ACT.Square).then_inc(sq_done, 1)

            def root(nn, job, c0):
                wait_taken(act, job)
                A(rstd[:, c0:], rstd[:, c0:], ACT.Sqrt).then_inc(root_done, 1)

            def modulate(nn, which, c0):
                for k in range(KD):
                    act.wait_ge(hx_done, nn * KD + k + 1)
                    for s in range(c0 // CTX, 2):
                        ins = A(h[:, k, s * CTX:(s + 1) * CTX], h[:, k, s * CTX:(s + 1) * CTX], ACT.Identity,
                                scale=amul[:, which, k, s:s + 1], bias=mod[:, 3 * which, k, s:s + 1])
                    ins.then_inc(h_done, 1)

            act.wait_ge(const_in, 48)
            A(csil[:].rearrange("p a b -> p (a b)"), c("c"), ACT.Silu).then_inc(csil_done, 1)
            for l in range(LAYERS):
                c0 = 0 if l == 0 else CTX
                last_moe = lambda k: (l - 1, "moe", (NEXP - 1) * MOE_JOBS + 2 * KF + k)
                if l:
                    for k in range(KD):
                        wait_taken(act, last_moe(k))
                act.dma_start(sm, ssm[l]).then_inc(ssm_in, 16)
                act.dma_start(dsk.rearrange("p a b -> p (a b)"), dskip[l]).then_inc(ssm_in, 16)
                squares(2 * l, 0, lambda k: None)
                act.wait_ge(ssm_in, 32 * (l + 1))
                A(t8[:, 0], s_("ldt"), ACT.Exp).then_inc(trig_out, 1)
                act.wait_ge(trig_in, 2 * l + 1)
                A(t8[:, 1], t8[:, 1], ACT.Exp).then_inc(trig_out, 1)
                act.wait_ge(trig_in, 2 * l + 2)
                A(t8[:, 4], t8[:, 2], ACT.Sin).then_inc(trig_out, 1)
                A(t8[:, 5], t8[:, 2], ACT.Sin, scale=0.5).then_inc(trig_out, 1)
                root(2 * l, (l, "ms1"), 0)
                act.wait_ge(mod_done, l + 1)
                modulate(2 * l, 0, 0)
                for m in range(KW):
                    wait_taken(act, (l, "u", m))
                act.dma_start(u_dram.rearrange("(t p) j c -> p t (j c)", p=P), up).then_inc(u_out, 16)
                act.wait_ge(u_out, 16 * (l + 1))
                for j in range(STEP):
                    act.dma_start(ug[j * GRP:(j + 1) * GRP],
                                  u_dram[:, j, :].rearrange("(g h) c -> h g c", h=GRP)).then_inc(ug_in, 16)
                for q in range(NQ):
                    for r in range(2):
                        job = (l, "wt", q, r)
                        wait_full(act, job)
                        if q:
                            wait_full(act, (l, "st", q - 1))
                        free(job, nc.scalar.copy(wt[:, r].rearrange("p g n -> p (g n)"), bank(job)))
                for m in range(KW):
                    copy((l, "qa", m), qa[:, m, c0:], bank((l, "qa", m))[:, c0:])
                copy((l, "ka"), ka[:], bank((l, "ka")))
                copy((l, "va"), va[:].rearrange("p t n -> p (t n)"), bank((l, "va")))
                for m in range(KW):
                    job = (l, "qn", m)
                    wait_full(act, job)
                    free(job, nc.scalar.mul(qn[:, m, c0:], bank(job)[:, c0:], HD ** -0.5))
                for m in range(KW):
                    copy((l, "kn", m), kn[:, m, :], bank((l, "kn", m)))
                for t in range(NTOK // P):
                    copy((l, "vn", t), vn[:, t, :], bank((l, "vn", t)))
                for m in range(KW + 1):
                    t = c0 if m < KW else 0
                    src = qa[:, m, t:] if m < KW else ka[:, t:]
                    if m == 0:
                        for mm_ in range(KW):
                            wait_taken(act, (l, "qa", mm_))
                        wait_taken(act, (l, "ka"))
                    else:
                        wait_full(act, (l, "qk_ms", m - 1))
                    A(qsq[:, t:], src, ACT.Square).then_inc(qsq_done, 1)
                    wait_taken(act, (l, "qk_ms", m))
                    A(qrs[:, t:], qrs[:, t:], ACT.Sqrt).then_inc(qroot_done, 1)
                for q in range(NQ):
                    if q:
                        act.wait_ge(tm_in, 16 * STEP * (l * NQ + q))
                    for n in range(2):
                        job = (l, "z", q, n)
                        copy(job, zs[:, 2 * n:2 * n + 2].rearrange("p g n -> p (g n)"), bank(job)[0:GRP, 0:480])
                    act.wait_ge(zd_done, l * NQ + q + 1)
                    if q >= 2:
                        wait_full(act, (l, "y", q - 2))
                    for j in range(STEP):
                        a = (STEP - 1 - j) * GRP
                        act.dma_start(tm[j * GRP:(j + 1) * GRP, q % 2], zs[:, :, a:a + P]).then_inc(tm_in, 16)
                    if q:
                        copy((l, "y", q - 1), ug[:, (q - 1) * GQ:q * GQ].rearrange("p g c -> p (g c)"),
                             bank((l, "y", q - 1))[:, 0:GQ * NCH])
                copy((l, "y", NQ - 1), ug[:, (NQ - 1) * GQ:].rearrange("p g c -> p (g c)"),
                     bank((l, "y", NQ - 1))[:, 0:GQ * NCH])
                for q in range(NQ):
                    wait_taken(act, (l, "y", q))
                for j in range(STEP):
                    act.dma_start(y_dram[:, j, :].rearrange("(g h) c -> h g c", h=GRP),
                                  ug[j * GRP:(j + 1) * GRP]).then_inc(y_out, 16)
                act.wait_ge(y_out, 16 * STEP * (l + 1))
                act.dma_start(yt, y_dram.rearrange("(t p) j c -> p t (j c)", p=P)).then_inc(y_in, 16)
                for r in range(GRID_H):
                    for rk in range(GRID_H):
                        row = l * HEADS * RPB_ROWS + RPB_ROWS // 2 + rk - r
                        act.dma_start(
                            bias[(r % 2) * GRID_W:(r % 2 + 1) * GRID_W, r // 2, :, rk],
                            bass.AP(tensor=rpb.tensor, offset=row * GRID_W * RPB_PAD + GRID_W - 1,
                                    ap=[[RPB_PAD - 1, GRID_W], [RPB_ROWS * GRID_W * RPB_PAD, HEADS], [1, GRID_W]]))\
                            .then_inc(bias_in, 16)
                us = units[l]
                for n in range(len(us) + 4):
                    if n < len(us):
                        N, nk = n_before[l] + n, us[n][4]
                        act.wait_ge(max_done, N + 1)
                        if N >= 3:
                            act.wait_ge(turn_full[(N - 3) % 2], (N - 3) // 2 + 1)
                        free((l, "sc", n),
                             A(probs[:, N % 3, 0:nk], bank((l, "sc", n))[:, 0:nk], ACT.Exp,
                               bias=smx[:, 0, N % 64:N % 64 + 1], accum_out=smx[:, 1, N % 64:N % 64 + 1]))
                    if n >= 4 and us[n - 4][2:4] == (1, NTOK - P):
                        br, i = us[n - 4][0:2]
                        O = (l * 2 + br) * KW + i
                        act.wait_ge(out_full[O % 2], O // 2 + 1)
                        nc.scalar.copy(bo[1 + br][:, i, c0:], out_ps[:, O % 2, c0:]).then_inc(out_free[O % 2], 1)
                act.wait_ge(y_in, 16 * (l + 1))
                for t in range(KW):
                    src = yt[:, t].rearrange("p (j c) -> p c j", j=STEP)[:, c0 // STEP:, :]
                    A(z[:, t, c0:].rearrange("p (c j) -> p c j", j=STEP), src, ACT.Gelu_apprx_tanh)\
                        .then_inc(gelu_done, 1)
                for m in range(KW):
                    if m >= 2:
                        act.wait_ge(glu_done, l * KW + m - 1)
                    job = (l, "glu", m)
                    wait_full(act, job)
                    free(job, A(sig[:, m % 2, c0:], bank(job)[:, c0:], ACT.Sigmoid))
                act.wait_ge(glu_done, (l + 1) * KW)
                order = [(l, "br", hf, b, m) for hf in range(2) for b in range(3) for m in range(KW)]
                for n, (_, _, hf, b, m) in enumerate(order):
                    if n >= 2:
                        wait_taken(act, order[n - 2])
                    job = (l, "gate", hf, b, m)
                    wait_full(act, job)
                    free(job, A(sig[:, n % 2, c0:], bank(job)[:, c0:], ACT.Sigmoid))
                squares(2 * l + 1, c0, lambda k: wait_taken(act, (l, "wo", k)))
                root(2 * l + 1, (l, "ms2"), c0)
                modulate(2 * l + 1, 1, c0)
                act.wait_ge(rl_done, l + 1)
                A(rt[:, 3, c0 // P:], rt[:, 2, c0 // P:], ACT.Exp).then_inc(re_done, 1)
                for e in range(NEXP):
                    copy((l, "comb", e), comb_bc[:, e, c0:], bank((l, "comb", e))[:, c0:])
                with act.Fori(0, NEXP) as i:
                    for f in range(KF):
                        job = (l, "moe", 2 * f)
                        wait_full(act, job, i * (MOE_JOBS // BANKS))
                        if f >= 2:
                            act.wait_ge(hid_done, i * KF + l * NEXP * KF + f - 1)
                        free(job, A(act_g[:, f % 2, c0:], bank(job)[:, c0:], ACT.Silu))
            squares(2 * LAYERS, CTX, lambda k: wait_taken(act, (LAYERS - 1, "moe", (NEXP - 1) * MOE_JOBS + 2 * KF + k)))
            root(2 * LAYERS, (LAYERS, "ms"), CTX)

        def into_steps(dve, link, l, q):
            job = (l, "st", q)
            gs = slice(q * GQ, (q + 1) * GQ)
            v = bank(job).rearrange("p (g r c) -> p r g c", r=2, c=NCH)
            wait_full(dve, job)
            dve.tensor_copy(st[0:NST, :, gs, 1:], v[0:NST])
            dve.tensor_copy(st[NST:P, :, gs, 1:NCC + 1][:, :, :, ::-1], v[NST:P, :, :, 0:NCC])
            free(job, dve.tensor_copy(st[NST:P, :, gs, NCC + 1:][:, :, :, ::-1], v[NST:P, :, :, NCC:]))

        @block.vector
        def _(dve):
            link = Link(dve, dve_link)
            TT, TS, STT, CP = dve.tensor_tensor, dve.tensor_scalar, dve.scalar_tensor_tensor, dve.tensor_copy

            def discretise(l):
                lre, lim = s_("lre"), s_("lim")
                dt, er, th, n = (t8[:, k] for k in range(4))
                dve.wait_ge(ssm_in, 32 * (l + 1))
                dve.wait_ge(trig_out, 4 * l + 1)
                TT(er, lre, dt, ALU.mult).then_inc(trig_in, 1)
                link(TT(th, lim, dt, ALU.mult))
                link(TS(n, th, 1 / (2 * math.pi), ROUND, ALU.mult, ALU.add))
                link(TS(n, n, ROUND, None, ALU.subtract))
                for part in (TWO_PI_1, TWO_PI_2, TWO_PI_3):
                    link(STT(th, n, -part, th, ALU.mult, ALU.add))
                TS(th, th, PI_BELOW, -PI_BELOW, ALU.min, ALU.max).then_inc(trig_in, 1)
                link(dve.memset(pw[:, 0, 0], 1.0))
                link(dve.memset(pw[:, 1, 0], 0.0))
                link(dve.memset(pws, 0.0))
                link(dve.memset(st[:, :, :, 0], 0.0))
                dve.wait_ge(trig_out, 4 * l + 4)
                sn, sh, cs = t8[:, 4], t8[:, 5], t8[:, 6]
                link(TT(cs, sh, sh, ALU.mult))
                link(TS(cs, cs, -2.0, 1.0, ALU.mult, ALU.add))
                ar, ai = pw[:, 0, 1], pw[:, 1, 1]
                link(TT(ar, er, cs, ALU.mult))
                link(TT(ai, er, sn, ALU.mult))
                inv, am, nr, ni, tmp = (t8[:, k] for k in range(7, 12))
                link(TT(inv, lre, lre, ALU.mult))
                link(TT(tmp, lim, lim, ALU.mult))
                link(TT(inv, inv, tmp, ALU.add))
                link(dve.reciprocal(inv, inv))
                link(TS(am, ar, 1.0, None, ALU.subtract))
                link(TT(nr, am, lre, ALU.mult))
                link(TT(tmp, ai, lim, ALU.mult))
                link(TT(nr, nr, tmp, ALU.add))
                link(TT(nr, nr, inv, ALU.mult))
                link(TT(ni, ai, lre, ALU.mult))
                link(TT(tmp, am, lim, ALU.mult))
                link(TT(ni, ni, tmp, ALU.subtract))
                link(TT(ni, ni, inv, ALU.mult))
                bre, bim = (s_(k).rearrange("p (g h) -> p g h", h=GRP) for k in ("bre", "bim"))
                nrb, nib = spread(nr, 2, GRP), spread(ni, 2, GRP)
                tb = wtmp.rearrange("p a b c -> p (a b c)")[:, 0:NGRP * GRP].rearrange("p (g h) -> p g h", h=GRP)
                link(TT(bb[:, 0], bre, nrb, ALU.mult))
                link(TT(tb, bim, nib, ALU.mult))
                link(TT(bb[:, 0], bb[:, 0], tb, ALU.subtract))
                link(TT(bb[:, 1], bim, nrb, ALU.mult))
                link(TT(tb, bre, nib, ALU.mult))
                link(TT(bb[:, 1], bb[:, 1], tb, ALU.add))
                for n in (1, 2, 4):
                    lo, hi = slice(1, n + 1), slice(n + 1, 2 * n + 1)
                    fr, fi = spread(pw[:, 0, n], 1, n), spread(pw[:, 1, n], 1, n)
                    tp = sst.rearrange("p a b g -> p (a b) g")[:, 0:n]
                    link(TT(pw[:, 0, hi], pw[:, 0, lo], fr, ALU.mult))
                    link(TT(tp, pw[:, 1, lo], fi, ALU.mult))
                    link(TT(pw[:, 0, hi], pw[:, 0, hi], tp, ALU.subtract))
                    link(TT(pw[:, 1, hi], pw[:, 0, lo], fi, ALU.mult))
                    link(TT(tp, pw[:, 1, lo], fr, ALU.mult))
                    link(TT(pw[:, 1, hi], pw[:, 1, hi], tp, ALU.add))
                F, B = slice(0, NST), slice(NST, P)
                link(CP(pww[F], pw[F, :, 0:STEP][:, :, ::-1]))
                link(CP(pww[B], pw[B, :, 0:STEP]))
                for d, at in ((F, slice(STEP, NPOS)), (B, slice(0, STEP + 1))):
                    for r, sign in ((0, 1.0), (1, -1.0)):
                        src = pw[d, r] if d is F else pw[d, r][:, ::-1]
                        link(TS(pws[d, r, at], src, sign, None, ALU.mult))
                a8r, a8i = pw[:, 0, STEP], pw[:, 1, STEP]
                link(CP(a8s[:, 0], spread(a8r, 1, 2)))
                link(TS(a8s[:, 1, 0], a8i, -1.0, None, ALU.mult))
                CP(a8s[:, 1, 1], a8i).then_inc(pow_done, 1)
                dve.wait_ge(pow_done, l + 1)

            def rms(nn, job, c0):
                wait_full(dve, job)
                free(job, TS(rstd[:, c0:], bank(job)[:, c0:], EPS, None, ALU.add))
                dve.wait_ge(root_done, nn + 1)
                link(dve.reciprocal(rstd[:, c0:], rstd[:, c0:]))

            def normalise(nn, c0):
                for k in range(KD):
                    TT(h[:, k, c0:], x[:, k, c0:], rstd[:, c0:], ALU.mult).then_inc(hx_done, 1)

            def route(l, c0):
                t0 = c0 // P
                T = NTOK // P - t0
                R = lambda k, n=NEXP: rt[:, k, t0:, 0:n]
                col = lambda k: rt[:, k, t0:, 0:1]

                def wide(v, n):
                    return v.broadcast_to([P, T, n])

                def first_max(out, src, n, m, tmp):
                    link(dve.tensor_reduce(col(m), src, AX.X, ALU.max))
                    link(TT(R(tmp, n), src, wide(col(m), n), ALU.is_equal))
                    iota = spread(c("iota")[:, 0:n], 1, T)
                    link(STT(R(tmp, n), R(tmp, n), -64.0, iota, ALU.mult, ALU.add))
                    link(dve.tensor_reduce(col(m), R(tmp, n), AX.X, ALU.min))
                    link(TT(out, R(tmp, n), wide(col(m), n), ALU.is_equal))

                job = (l, "rt")
                wait_full(dve, job)
                free(job, CP(R(0), bank(job)[:, t0 * NEXP:(NTOK // P) * NEXP].rearrange("p (t e) -> p t e", e=NEXP)))
                wait_taken(dve, job)
                link(dve.tensor_reduce(col(1), R(0), AX.X, ALU.max))
                TT(R(2), R(0), wide(col(1), NEXP), ALU.subtract).then_inc(rl_done, 1)
                dve.wait_ge(re_done, l + 1)
                link(dve.tensor_reduce(col(4), R(3), AX.X, ALU.add))
                link(dve.reciprocal(col(5), col(4)))
                link(TT(R(6), R(3), wide(col(5), NEXP), ALU.mult))
                link(TT(R(7), R(6), spread(c("rb"), 1, T), ALU.add))
                s4 = R(7).rearrange("p t (g e) -> p t g e", e=EGRP)
                one = lambda e: s4[:, :, :, e]
                Q = lambda k: R(k, EGRP)
                link(TT(Q(8), one(0), one(1), ALU.max))
                link(TT(Q(9), one(0), one(1), ALU.min))
                link(TT(Q(10), one(2), one(3), ALU.max))
                link(TT(Q(11), one(2), one(3), ALU.min))
                link(TT(Q(12), Q(8), Q(10), ALU.max))
                link(TT(Q(13), Q(8), Q(10), ALU.min))
                link(TT(Q(14), Q(9), Q(11), ALU.max))
                link(TT(Q(13), Q(13), Q(14), ALU.max))
                link(TT(Q(15), Q(12), Q(13), ALU.add))
                first_max(Q(16), Q(15), EGRP, 17, 18)
                in_g = spread(Q(16), 3, EGRP)
                r19 = R(19).rearrange("p t (g e) -> p t g e", e=EGRP)
                r20 = R(20).rearrange("p t (g e) -> p t g e", e=EGRP)
                link(TS(r19, in_g, FAR, FAR, ALU.mult, ALU.subtract))
                link(TT(r20, s4, in_g, ALU.mult))
                link(TT(R(20), R(20), R(19), ALU.add))
                first_max(R(21), R(20), NEXP, 17, 18)
                link(STT(R(20), R(21), -3 * FAR, R(20), ALU.mult, ALU.add))
                first_max(R(22), R(20), NEXP, 17, 18)
                link(TT(R(21), R(21), R(22), ALU.add))
                link(TT(R(6), R(6), R(21), ALU.mult))
                link(dve.tensor_reduce(col(4), R(6), AX.X, ALU.add))
                link(dve.reciprocal(col(5), col(4)))
                TT(R(COMB), R(6), wide(col(5), NEXP), ALU.mult).then_inc(comb_done, 1)

            dve.wait_ge(const_in, 48)
            for l in range(LAYERS):
                c0 = 0 if l == 0 else CTX
                segs = range(c0 // CTX, 2)
                ms = lambda k: mis[:, l, MISC[k]]
                discretise(l)
                job = (l, "mod")
                wait_full(dve, job)
                free(job, TT(mod[:].rearrange("p a k s -> p (a k) s"), bank(job)[:, 0:96].rearrange("p (a s) -> p a s", s=2),
                             spread(ms("bmod"), 2, 2), ALU.add))
                wait_taken(dve, job)
                link(STT(amul[:, 0], mod[:, 1], 1.0, spread(ms("n1"), 2, 2), ALU.add, ALU.mult))
                link(STT(amul[:, 1], mod[:, 4], 1.0, spread(ms("n2"), 2, 2), ALU.add, ALU.mult))
                TS(qg8[:], ms("qg"), HD ** -0.5, None, ALU.mult).then_inc(mod_done, 1)
                dve.wait_ge(mod_done, l + 1)
                rms(2 * l, (l, "ms1"), 0)
                normalise(2 * l, 0)
                for m in range(KW):
                    job = (l, "u", m)
                    wait_full(dve, job)
                    free(job, CP(up[:, m].rearrange("p (j c) -> p j c", j=STEP),
                                 bank(job).rearrange("p (c j) -> p j c", j=STEP)))
                for q in range(NQ):
                    gs = slice(q * GQ, (q + 1) * GQ)
                    if q:
                        wait_full(dve, (l, "wt", q - 1, 1))
                    pv = [spread(pww[:, r, :, gs].rearrange("p j g -> p g j"), 3, GRP) for r in range(2)]
                    bv = [spread(bb[:, r, gs, :], 2, STEP) for r in range(2)]
                    link(TT(wm[:, 0], pv[0], bv[0], ALU.mult))
                    link(TT(wtmp, pv[1], bv[1], ALU.mult))
                    link(TT(wm[:, 0], wm[:, 0], wtmp, ALU.subtract))
                    link(TT(wm[:, 1], pv[0], bv[1], ALU.mult))
                    link(TT(wtmp, pv[1], bv[0], ALU.mult))
                    TT(wm[:, 1], wm[:, 1], wtmp, ALU.add).then_inc(wm_done, 1)
                    if q:
                        into_steps(dve, link, l, q - 1)
                into_steps(dve, link, l, NQ - 1)
                wait_taken(dve, (l, "st", NQ - 1))
                with dve.Fori(0, NCH) as i:
                    now = st[:, :, :, bass.ds(i, 1)].rearrange("p r g s -> p r (g s)")
                    nxt = st[:, :, :, bass.ds(i + 1, 1)].rearrange("p r g s -> p r (g s)")
                    if l:
                        dve.wait_ge(scan_done, i + l * NCH)
                    TT(sst[:, 0], now, a8s[:, 0], ALU.mult)
                    TT(sst[:, 1, 0], now[:, 1], a8s[:, 1, 0], ALU.mult)
                    link(TT(sst[:, 1, 1], now[:, 0], a8s[:, 1, 1], ALU.mult), i * 2)
                    link(TT(nxt, nxt, sst[:, 0], ALU.add), i * 2)
                    TT(nxt, nxt, sst[:, 1], ALU.add).then_inc(scan_done, 1)
                    dve.wait_ge(scan_done, i + (l * NCH + 1))
                link.n += 2 * (NCH - 1)
                for m in range(KW + 1):
                    t = c0 if m < KW else 0
                    v, g = (qa[:, m], qg8[:, 0:1]) if m < KW else (ka[:, :], ms("kg"))
                    n = l * (KW + 1) + m + 1
                    job = (l, "qk_ms", m)
                    wait_full(dve, job)
                    free(job, TS(qrs[:, t:], bank(job)[:, t:], EPS, None, ALU.add))
                    dve.wait_ge(qroot_done, n)
                    link(dve.reciprocal(qrs[:, t:], qrs[:, t:]))
                    STT(v[:, t:], v[:, t:], g, qrs[:, t:], ALU.mult, ALU.mult).then_inc(qnorm_done, 1)
                    dve.wait_ge(qnorm_done, n)
                    job = (l, "rope", m)
                    wait_full(dve, job)
                    free(job, TT(qrt[:], bank(job)[:, 0:LAT], c("sin"), ALU.mult))
                    link(TT(v[:, CTX:], v[:, CTX:], c("cos"), ALU.mult))
                    wait_taken(dve, job)
                    TT(v[:, CTX:], v[:, CTX:], qrt[:], ALU.add).then_inc(rope_done, 1)
                for q in range(NQ):
                    for n in range(2):
                        wait_taken(dve, (l, "z", q, n))
                    mid = slice((STEP - 1) * GRP, STEP * GRP)
                    TT(zs[:, :, mid], zs[:, :, mid], dsk[:, q * GQ:(q + 1) * GQ, :], ALU.add).then_inc(zd_done, 1)
                us = units[l]
                for n in range(len(us) + 3):
                    if n < len(us):
                        br, i, half, q0, nk = us[n]
                        job = (l, "sc", n)
                        wait_full(dve, job)
                        if br == 1 and q0 >= CTX:
                            dve.wait_ge(bias_done, 2 * (l + 1))
                            v = bank(job)[:, CTX:NTOK]
                            b = bias[:, (q0 - CTX) // P, 2 * i + half].rearrange("p r c -> p (r c)")
                            link(TT(v, v, b, ALU.add))
                        N = n_before[l] + n
                        dve.tensor_reduce(smx[:, 0, N % 64:N % 64 + 1], bank(job)[:, 0:nk], AX.X, ALU.max,
                                          negate=True).then_inc(max_done, 1)
                    if 1 <= n <= len(us):
                        N = n_before[l] + n - 1
                        wait_taken(dve, (l, "sc", n - 1))
                        dve.reciprocal(smx[:, 2, N % 64:N % 64 + 1], smx[:, 1, N % 64:N % 64 + 1]).then_inc(inv_done, 1)
                    if n >= 3:
                        N, nk = n_before[l] + n - 3, us[n - 3][4]
                        dve.wait_ge(turn_full[N % 2], N // 2 + 1)
                        CP(pt[:, N % 2, 0:nk // P].rearrange("p t n -> p (t n)"), turn_ps[:, N % 2, 0:nk])\
                            .then_inc(turn_free[N % 2], 1)
                dve.wait_ge(gelu_done, (l + 1) * KW)
                for m in range(KW):
                    wait_taken(dve, (l, "glu", m))
                    TT(bo[0][:, m, c0:], z[:, m, c0:], sig[:, m % 2, c0:], ALU.mult).then_inc(glu_done, 1)
                mixed = 4 * KW * l
                for n, (hf, b, m) in enumerate((hf, b, m) for hf in range(2) for b in range(3) for m in range(KW)):
                    job = (l, "br", hf, b, m)
                    wait_taken(dve, (l, "gate", hf, b, m))
                    wait_full(dve, job)
                    s, out = sig[:, n % 2, c0:], mg[:, hf * KW + m, c0:]
                    if b == 0:
                        free(job, TT(out, bank(job)[:, c0:], s, ALU.mult))
                    else:
                        v = prod[:, mixed % 2, c0:]
                        if mixed >= 2:
                            dve.wait_ge(mix_done, mixed - 1)
                        free(job, TT(v, bank(job)[:, c0:], s, ALU.mult))
                        wait_taken(dve, job)
                        if b == 1:
                            wait_taken(dve, (l, "br", hf, 0, m))
                        else:
                            dve.wait_ge(mix_done, mixed - KW + 1)
                        TT(out, out, v, ALU.add).then_inc(mix_done, 1)
                        mixed += 1
                for m in range(KD):
                    job = (l, "wo", m)
                    wait_full(dve, job)
                    if l:
                        wait_taken(dve, (l - 1, "moe", (NEXP - 1) * MOE_JOBS + 2 * KF + m))
                    for s in segs:
                        t = slice(s * CTX, (s + 1) * CTX)
                        ins = STT(x[:, m, t], bank(job)[:, t], mod[:, 2, m, s:s + 1], x[:, m, t], ALU.mult, ALU.add)
                    free(job, ins)
                for m in range(KD):
                    wait_taken(dve, (l, "wo", m))
                rms(2 * l + 1, (l, "ms2"), c0)
                normalise(2 * l + 1, c0)
                route(l, c0)
                wait_taken(dve, (l, "comb", NEXP - 1))
                for e in range(NEXP - 4, NEXP):
                    wait_taken(dve, (l, "comb", e))
                with dve.Fori(0, NEXP) as i:
                    more = i * (MOE_JOBS // BANKS)
                    share = comb_bc[:, bass.ds(i, 1), c0:].rearrange("p e n -> p (e n)")
                    for f in range(KF):
                        job = (l, "moe", 2 * f + 1)
                        wait_full(dve, job, more)
                        if f >= 2:
                            dve.wait_ge(hid_done, i * KF + (l * NEXP * KF + f - 1))
                        free(job, TT(act_u[:, f % 2, c0:], bank(job)[:, c0:], share, ALU.mult))
                        wait_taken(dve, job, more)
                        wait_taken(dve, (l, "moe", 2 * f), more)
                        TT(hid[:, f, c0:], act_g[:, f % 2, c0:], act_u[:, f % 2, c0:], ALU.mult).then_inc(hid_done, 1)
                    for m in range(KD - BANKS, KD):
                        wait_bank(dve, (l, "moe", m - (KD - BANKS)), more)
                    for m in range(KD):
                        job = (l, "moe", 2 * KF + m)
                        wait_full(dve, job, more)
                        for s in segs:
                            t = slice(s * CTX, (s + 1) * CTX)
                            ins = STT(x[:, m, t], bank(job)[:, t], mod[:, 5, m, s:s + 1], x[:, m, t],
                                      ALU.mult, ALU.add)
                        free(job, ins)
            for m in range(KD):
                wait_taken(dve, (LAYERS - 1, "moe", (NEXP - 1) * MOE_JOBS + 2 * KF + m))
            rms(2 * LAYERS, (LAYERS, "ms"), CTX)
            for k in range(KD):
                STT(h[:, k, CTX:], x[:, k, CTX:], c("fg")[:, k:k + 1], rstd[:, CTX:], ALU.mult, ALU.mult)\
                    .then_inc(fin_done, 1)

        @block.gpsimd
        def _(pool):
            link = Link(pool, pool_link)
            TT = pool.tensor_tensor
            pool.wait_ge(const_in, 48)
            for l in range(LAYERS):
                pool.wait_ge(pow_done, l + 1)
                wait_full(pool, (l, "st", NQ - 1))
                wait_full(pool, (l, "wt", NQ - 1, 1))
                cre, cim = (s_(k).rearrange("p (g h) -> p g h", h=GRP) for k in ("cre", "cim"))
                for q in range(NQ):
                    gs = slice(q * GQ, (q + 1) * GQ)
                    if q >= 2:
                        wait_full(pool, (l, "y", q - 2))
                    pv = [spread(pws[:, r, :, gs].rearrange("p n g -> p g n"), 3, GRP) for r in range(2)]
                    cv = [spread(v[:, gs], 2, NPOS) for v in (cre, cim)]
                    o0, o1 = (cp[:, r, (q % 2) * GQ:(q % 2 + 1) * GQ] for r in range(2))
                    link(TT(o0, pv[0], cv[0], ALU.mult))
                    link(TT(ctmp, pv[1], cv[1], ALU.mult))
                    link(TT(o0, o0, ctmp, ALU.add))
                    link(TT(o1, pv[1], cv[0], ALU.mult))
                    link(TT(ctmp, pv[0], cv[1], ALU.mult))
                    TT(o1, o1, ctmp, ALU.subtract).then_inc(cp_done, 1)
                    pool.wait_ge(cp_done, l * NQ + q + 1)
                us = units[l]
                for n in range(len(us)):
                    if n == len(us) // 4:
                        pool.wait_ge(bias_in, 16 * GRID_H ** 2 * (l + 1))
                        for qt in range(2):
                            b = bias[:, qt].rearrange("p h r c -> p (h r) c")
                            TT(b, b, spread(c("far_cols"), 1, HEADS * GRID_H), ALU.add).then_inc(bias_done, 1)
                    N, nk = n_before[l] + n, us[n][4]
                    pool.wait_ge(inv_done, N + 1)
                    v = probs[:, N % 3, 0:nk]
                    pool.tensor_scalar(v, v, smx[:, 2, N % 64:N % 64 + 1], None, ALU.mult).then_inc(prob_done, 1)


def constants(c, c_ctx, router_w, router_b, final_norm_g):
    out = np.zeros((P, N_CON), np.float32)
    out[:, CON["ident"]] = np.eye(P)
    out[:, CON["head_mean"]] = np.kron(np.eye(P // HD), np.full((HD, HD), 1 / HD))
    out[:, CON["model_mean"]] = 1 / D
    n_freq = HD // 4
    rot = np.zeros((P, P), np.float32)
    for a in range(0, P, 2 * n_freq):
        for f in range(n_freq):
            rot[a + n_freq + f, a + f] = -1
            rot[a + f, a + n_freq + f] = 1
    out[:, CON["rot"]] = rot
    t = np.arange(LAT)
    inv = np.float32(10000.0) ** (-np.arange(n_freq, dtype=np.float32) / np.float32(n_freq))
    ang = np.stack([(t // GRID_W).astype(np.float32)[:, None] * inv, (t % GRID_W).astype(np.float32)[:, None] * inv])
    by_channel = np.tile(np.repeat(ang[:, :, None, :], 2, 2).transpose(0, 2, 3, 1).reshape(HD, LAT), (2, 1))
    out[:, CON["cos"]], out[:, CON["sin"]] = np.cos(by_channel), np.sin(by_channel)
    out[:, CON["iota"]] = np.arange(NEXP)
    cq = np.arange(P)[:, None] % GRID_W
    ck = np.arange(GRID_W)[None]
    first = np.clip(cq - WIN_W // 2, 0, GRID_W - WIN_W)
    out[:, CON["far_cols"]] = np.where((ck >= first) & (ck < first + WIN_W), 0, -FAR)
    out[:, CON["rw"]] = router_w.reshape(KD, P, NEXP).transpose(1, 0, 2).reshape(P, -1)
    out[:, CON["rb"]] = router_b
    out[:, CON["fg"]] = final_norm_g.reshape(KD, P).T
    out[:, CON["c"]] = np.stack([c_ctx, c[0]], -1).reshape(KD, P, 2).transpose(1, 0, 2).reshape(P, -1)
    return out


def pack_weights(w_mod, w_in, ssm_w_glu, w_branch, w_out, moe_w_gate, moe_w_up, moe_w_down):
    def by_col(w):
        n = w.shape[1] // 256
        return w.reshape(KD, P, n, 256).transpose(2, 1, 0, 3).reshape(n, P, SLOT)

    def by_half(w):
        n = w.shape[1] // 512
        return w.reshape(KW, P, n, 512).transpose(2, 1, 0, 3).reshape(n, P, SLOT)

    pair = np.arange(WID).reshape(2, KW, HD).transpose(1, 0, 2).reshape(-1)
    slots = []
    for l in range(LAYERS):
        w = w_in[l]
        slots += [by_col(w_mod[l]), by_col(w[:, 0:512]), by_col(w[:, 512:1024][:, pair]),
                  by_col(w[:, 1024:2816])]
        slots.append(by_half(ssm_w_glu[l]))
        gates = [by_col(w[:, 2816 + b * D:2816 + (b + 1) * D]) for b in range(3)]
        branch = [by_half(w_branch[l, 0]), by_half(w_branch[l, 1][pair]), by_half(w_branch[l, 2])]
        for hf in range(2):
            for b in range(3):
                slots += [gates[b][2 * hf:2 * hf + 1], branch[b][hf:hf + 1], gates[b][2 * hf + 1:2 * hf + 2]]
        slots.append(by_col(w_out[l]))
        for e in range(NEXP):
            g, u, d = by_col(moe_w_gate[l, e]), by_col(moe_w_up[l, e]), by_half(moe_w_down[l, e])
            slots += [g[0:1], u[0:1], g[1:2], u[1:2], d]
    return np.concatenate(slots)


def kernel(x, c, ctx, c_ctx, w_mod, b_mod, norm1_g, norm2_g, w_in,
           ssm_lam_re, ssm_lam_im, ssm_log_dt, ssm_b_re, ssm_b_im, ssm_c_re, ssm_c_im,
           ssm_d, ssm_w_glu, gqa_q_norm_g, gqa_k_norm_g, na_rpb, w_branch, w_out,
           router_w, router_b, moe_w_gate, moe_w_up, moe_w_down, final_norm_g):
    import concourse.bacc as bacc
    from concourse.bass_utils import run_bass_kernel_spmd

    f32 = np.float32
    lay = {}
    lay["xT"] = np.concatenate([ctx[0], x[0]]).T
    lay["wpack"] = pack_weights(*(np.asarray(w) for w in (w_mod, w_in, ssm_w_glu, w_branch, w_out,
                                                           moe_w_gate, moe_w_up, moe_w_down)))
    tiles = lambda v: np.asarray(v).reshape(LAYERS, -1, P).transpose(0, 2, 1)
    twice = lambda v: np.tile(np.asarray(v), (1, P // HD))[:, :, None]
    lay["misc"] = np.concatenate([tiles(b_mod), tiles(norm1_g), tiles(norm2_g), twice(gqa_q_norm_g),
                                  twice(gqa_k_norm_g)], 2)
    state = lambda v: np.asarray(v).transpose(0, 1, 3, 2).reshape(LAYERS, P, NGRP)
    ldt = np.repeat(np.asarray(ssm_log_dt)[:, :, None, :], NST, 2).reshape(LAYERS, P, NGRP)
    b_lay = lambda v: np.asarray(v).transpose(0, 1, 3, 2, 4).reshape(LAYERS, P, NGRP * GRP)
    c_lay = lambda v: np.asarray(v).transpose(0, 1, 4, 2, 3).reshape(LAYERS, P, NGRP * GRP)
    lay["ssm"] = np.concatenate([state(ssm_lam_re), state(ssm_lam_im), ldt, b_lay(ssm_b_re), b_lay(ssm_b_im),
                                 c_lay(ssm_c_re), c_lay(ssm_c_im)], 2)
    dskip = np.zeros((LAYERS, GRP, NGRP, GRP), f32)
    for i in range(GRP):
        dskip[:, i, :, i] = np.asarray(ssm_d).reshape(LAYERS, NGRP, GRP)[:, :, i]
    lay["dskip"] = dskip.reshape(LAYERS, GRP, NGRP * GRP)
    rpb = np.zeros((LAYERS, HEADS, RPB_ROWS, RPB_PAD), f32)
    side = (RPB_PAD - RPB_COLS) // 2
    rpb[..., side:side + RPB_COLS] = na_rpb
    lay["rpb"] = np.repeat(rpb[:, :, :, None, :], GRID_W, 3)
    lay["const"] = constants(*(np.asarray(v) for v in (c, c_ctx, router_w, router_b, final_norm_g)))

    nc = bacc.Bacc("TRN2", target_bir_lowering=False, num_devices=1)
    arrays, args = {}, []
    for name, a in lay.items():
        arrays[f"in_{name}"] = np.ascontiguousarray(a)
        args.append(nc.dram_tensor(f"in_{name}", a.shape, F32, kind="ExternalInput").ap())
    args.append(nc.dram_tensor("outT", (D, LAT), F32, kind="ExternalOutput").ap())
    backbone(nc, *args)
    r = run_bass_kernel_spmd(nc, [arrays], core_ids=[0])
    return r.results[0]["outT"].T[None]
```

```python
import math
from contextlib import ExitStack

import numpy as np

import concourse.bass as bass
from concourse import mybir

F32 = mybir.dt.float32
ALU = mybir.AluOpType
ACT = mybir.ActivationFunctionType
AX = mybir.AxisListType

P = 128
D = 1024
KD = D // P
CTX, LAT = 256, 256
NTOK = CTX + LAT
LAYERS = 2
GRID_W = 64
GRID_H = LAT // GRID_W
HD = 64
HEADS = 8
WID = 512
KW = WID // P
WIN_W = 16
RPB_ROWS, RPB_COLS = 15, 31
RPB_PAD = 2 * GRID_W - 1
NGRP, GRP, NST = 32, 16, 64
STEP = P // GRP
NCH = NTOK // STEP
NCC = CTX // STEP
GQ = 4
NQ = NGRP // GQ
NPOS = 2 * STEP + 1
NEXP, EGRP = 16, 4
KF = 4
EPS = 1e-6
FAR = 1e30
ROUND = 12582912.0

SLOT = 2048
RING = 6
S_MOD, S_U, S_QA, S_KV, S_QN, S_KN, S_VN, S_GLU, S_MIX, S_OUT, S_MOE = (
    0, 24, 26, 28, 29, 31, 33, 35, 36, 54, 58)
PER_LAYER = S_MOE + NEXP * RING
TURNS = NEXP // 2
BS = 128



def columns(*sizes):
    at, out = 0, {}
    for name, n in sizes:
        out[name] = slice(at, at + n)
        at += n
    return out, at


MISC, N_MISC = columns(("bmod", 48), ("n1", KD), ("n2", KD), ("qg", 1), ("kg", 1))
SSM, N_SSM = columns(("lre", NGRP), ("lim", NGRP), ("ldt", NGRP), ("bre", NGRP * GRP), ("bim", NGRP * GRP),
                     ("cre", NGRP * GRP), ("cim", NGRP * GRP))
CON, N_CON = columns(("ident", P), ("head_mean", P), ("model_mean", P), ("rot", P), ("cos", LAT), ("sin", LAT),
                     ("iota", NEXP), ("far_cols", GRID_W), ("rw", KD * NEXP), ("rb", NEXP), ("fg", KD),
                     ("c", 2 * KD))
LATE, N_LATE = columns(("before", P), ("slots", NTOK))

TWO_PI_1 = 6.28125
TWO_PI_2 = float(np.float32(2 * math.pi - TWO_PI_1))
TWO_PI_3 = 2 * math.pi - TWO_PI_1 - TWO_PI_2
PI_BELOW = 3.1415925

R_PICK, R_SLOT, R_SHARE = 0, 22, 23
BANKS = 4


def attention_units(layer):
    return [(br, i, half, q0, CTX if q0 < CTX else NTOK)
            for br in range(2) for i in range(KW) for half in range(2)
            for q0 in range(0 if layer == 0 else CTX, NTOK, P)]


def tile_jobs():
    names = []
    for l in range(LAYERS):
        names += [(l, "mod"), (l, "ms1")]
        names += [(l, "u", m) for m in range(KW)]
        for q in range(NQ):
            names += [(l, "wt", q, 0), (l, "wt", q, 1), (l, "st", q)]
        names += [(l, "qa", m) for m in range(KW)] + [(l, "ka"), (l, "va")]
        names += [(l, "qn", m) for m in range(KW)] + [(l, "kn", m) for m in range(KW)]
        names += [(l, "vn", m) for m in range(KW)]
        for m in range(KW + 1):
            names += [(l, "qk_ms", m), (l, "rope", m)]
        for q in range(NQ + 1):
            names += [(l, "z", q, 0), (l, "z", q, 1)] if q < NQ else []
            names += [(l, "y", q - 1)] if q else []
        names += [(l, "sc", u) for u in range(len(attention_units(l)))]
        names += [(l, "glu", m) for m in range(KW)]
        for hf in range(2):
            for b in range(3):
                for m in range(KW):
                    names += [(l, "gate", hf, b, m), (l, "br", hf, b, m)]
        names += [(l, "wo", m) for m in range(KD)]
        names += [(l, "ms2"), (l, "rt")]
        names += [(l, "ht", t, n) for t in range(0 if l == 0 else CTX // P, NTOK // P) for n in range(2)]
        names += [(l, "rank")]
    names.append((LAYERS, "ms"))
    return {n: i for i, n in enumerate(names)}


JOB = tile_jobs()


class Link:

    def __init__(self, eng, sem):
        self.eng, self.sem, self.n = eng, sem, 0

    def __call__(self, ins, more=0):
        self.n += 1
        ins.then_inc(self.sem, 1)
        self.eng.wait_ge(self.sem, self.n + more)


def spread(ap, axis, n):
    v = ap.unsqueeze(axis)
    shape = list(v.shape)
    shape[axis] = n
    return v.broadcast_to(shape)


def backbone(nc, xT, wpack, misc, ssm, dskip, rpb, const, late, outT):
    ctx = ExitStack()
    with ctx:
        def sb(name, shape):
            return ctx.enter_context(nc.sbuf_tensor(name, shape, F32))

        def sem(name):
            return ctx.enter_context(nc.semaphore(name))

        def sems(name, n):
            return [sem(f"{name}{i}") for i in range(n)]

        u_dram = nc.dram_tensor("u_scratch", [WID, STEP, NCH], F32, kind="Internal").ap()
        y_dram = nc.dram_tensor("y_scratch", [WID, STEP, NCH], F32, kind="Internal").ap()

        x = sb("x", [P, KD, NTOK])
        h = sb("h", [P, KD, NTOK])
        ring = sb("ring", [P, RING, SLOT])
        con = sb("con", [P, N_CON])
        mis = sb("mis", [P, LAYERS, N_MISC])
        qa = sb("qa", [P, KW, NTOK])
        ka = sb("ka", [P, NTOK])
        va = sb("va", [P, NTOK // P, P])
        qn = sb("qn", [P, KW, NTOK])
        kn = sb("kn", [P, KW, NTOK])
        vn = sb("vn", [P, NTOK // P, WID])
        mod = sb("mod", [P, 6, KD, 2])
        amul = sb("amul", [P, 2, KD, 2])
        csil = sb("csil", [P, KD, 2])
        rstd = sb("rstd", [P, NTOK])
        qsq = sb("qsq", [P, NTOK])
        qrs = rstd
        qrt = sb("qrt", [P, LAT])
        qg8 = sb("qg8", [P, 1])
        smx = sb("smx", [P, 3, 64])
        tab = ctx.enter_context(nc.sbuf_tensor("tab", [P, 2 * NEXP + 1], mybir.dt.int32))
        ARENA = 20224
        arena = sb("arena", [P, ARENA])

        def cut(start, shape, parts=P):
            n = int(np.prod(shape))
            assert start + n <= ARENA, (start, shape)
            v = arena[0:parts, start:start + n]
            if len(shape) > 1:
                names = "abcd"[:len(shape)]
                v = v.rearrange(f"p ({' '.join(names)}) -> p {' '.join(names)}", **dict(zip(names, shape)))
            return v, start + n

        a0 = 0
        sm, a0 = cut(a0, [N_SSM])
        ug, a0 = cut(a0, [NGRP, NCH])
        st, a0 = cut(a0, [2, NGRP, NCH + 1])
        bb, a0 = cut(a0, [2, NGRP, GRP])
        pw, a0 = cut(a0, [2, STEP + 1, NGRP])
        pww, a0 = cut(a0, [2, STEP, NGRP])
        pws, a0 = cut(a0, [2, NPOS, NGRP])
        t8, a0 = cut(a0, [12, NGRP])
        sst, a0 = cut(a0, [2, 2, NGRP])
        a8s, a0 = cut(a0, [2, 2, NGRP])
        up, a1 = cut(a0, [KW, STEP * NCH])
        wm, a1 = cut(a1, [2, GQ, STEP, GRP])
        wt, a1 = cut(a1, [2, GQ, P])
        wtmp, a1 = cut(a1, [GQ, STEP, GRP])
        cp, a2 = cut(a0, [2, 2 * GQ, NPOS, GRP])
        ctmp, a2 = cut(a2, [GQ, NPOS, GRP])
        zs, a2 = cut(a2, [GQ, (NPOS - 2) * GRP], parts=GRP)
        tm, a2 = cut(a2, [2, GQ, P])
        dsk, a2 = cut(a2, [NGRP, GRP], parts=GRP)
        a3 = 0
        bo = [None] * 3
        for b in range(3):
            bo[b], a3 = cut(a3, [KW, NTOK])
        bias, a4 = cut(a3, [2, HEADS, GRID_H, GRID_W])
        probs, a5 = cut(a4, [3, NTOK])
        pt, a5 = cut(a5, [2, NTOK // P, P])
        yt, a5 = cut(a5, [KW, STEP * NCH])
        z, a5 = cut(a5, [KW, NTOK])
        mg, _ = cut(a3, [KD, NTOK])
        sig, a6 = cut(a4, [2, NTOK])
        prod, a6 = cut(a6, [2, NTOK])
        lat_, _ = cut(a5 - 2 * KW * NTOK, [N_LATE])
        ht, a7 = cut(0, [NTOK // P, D])
        rt, a7 = cut(a7, [24, NTOK // P, NEXP])
        sel, a7 = cut(a7, [NTOK // P, BS])
        selw, a7 = cut(a7, [NTOK // P, BS])
        hs, a7 = cut(a7, [KD, BS])
        sg, a7 = cut(a7, [KF, BS])
        hid, a7 = cut(a7, [KF, BS])
        yT, a7 = cut(a7, [KD, BS])
        ys, a7 = cut(a7, [D])
        sw, a7 = cut(a7, [NTOK])
        assert a7 <= a5 - 2 * KW * NTOK
        twin = [v[:].rearrange("p k n -> p (k n)") for v in (qa, qn, kn, vn)]
        twin += [arena[:, ARENA - k * SLOT:ARENA - (k - 1) * SLOT] for k in (2, 1)]

        tile_ps = ctx.enter_context(nc.psum_tensor("tile_ps", [P, BANKS, 512], F32))
        turn_ps = ctx.enter_context(nc.psum_tensor("turn_ps", [P, 2, 512], F32))
        out_ps = ctx.enter_context(nc.psum_tensor("out_ps", [P, 2, 512], F32))

        const_in = sem("const_in")
        slot_in = sems("slot_in", RING)
        slot_used = sem("slot_used")
        tile_full, tile_free = sems("tile_full", BANKS), sems("tile_free", BANKS)
        turn_full, turn_free = sems("turn_full", 2), sems("turn_free", 2)
        out_full, out_free = sems("out_full", 2), sems("out_free", 2)
        dve_link, act_link, pool_link = sem("dve_link"), sem("act_link"), sem("pool_link")
        csil_done, mod_done = sem("csil_done"), sem("mod_done")
        sq_done, root_done, hx_done, h_done = sem("sq_done"), sem("root_done"), sem("hx_done"), sem("h_done")
        ssm_in = sem("ssm_in")
        u_out, ug_in, y_out, y_in = sem("u_out"), sem("ug_in"), sem("y_out"), sem("y_in")
        wm_done, scan_done = sem("wm_done"), sem("scan_done")
        trig_in, trig_out = sem("trig_in"), sem("trig_out")
        pow_done, cp_done, zd_done, tm_in = sem("pow_done"), sem("cp_done"), sem("zd_done"), sem("tm_in")
        qsq_done, qroot_done, qnorm_done, rope_done = (
            sem("qsq_done"), sem("qroot_done"), sem("qnorm_done"), sem("rope_done"))
        bias_in, bias_done = sem("bias_in"), sem("bias_done")
        max_done, inv_done, prob_done = sem("max_done"), sem("inv_done"), sem("prob_done")
        gelu_done, glu_done, mix_done = sem("gelu_done"), sem("glu_done"), sem("mix_done")
        rl_done, re_done, chosen, route_done, late_in = (
            sem("rl_done"), sem("re_done"), sem("chosen"), sem("route_done"), sem("late_in"))
        twin_in = sems("twin_in", RING)
        per_block = lambda name: [sem(f"{name}_{l}") for l in range(LAYERS)]
        eq_done, sel_done = per_block("eq_done"), per_block("sel_done")
        gather_full, hs_done = per_block("gather_full"), per_block("hs_done")
        gu_full, sg_done, hid_done = per_block("gu_full"), per_block("sg_done"), per_block("hid_done")
        down_full, yT_done = per_block("down_full"), per_block("yT_done")
        yt_full, ys_done = per_block("yt_full"), per_block("ys_done")
        w_full, sw_done = per_block("w_full"), per_block("sw_done")
        add_full = [sems(f"add_full{l}_", 2) for l in range(LAYERS)]
        add_done = [sems(f"add_done{l}_", 2) for l in range(LAYERS)]
        fin_done, stored = sem("fin_done"), sem("stored")

        def c(name):
            return con[:, CON[name]]

        def s_(name):
            return sm[:, SSM[name]]

        def bank(job):
            return tile_ps[:, JOB[job] % BANKS, :]

        def wait_full(eng, job, beyond=0):
            n = JOB[job]
            eng.wait_ge(tile_full[n % BANKS], n // BANKS + 1 + beyond)

        def wait_taken(eng, job, beyond=0):
            n = JOB[job]
            eng.wait_ge(tile_free[n % BANKS], n // BANKS + 1 + beyond)

        def wait_bank(pe, job, beyond=0):
            n = JOB[job]
            if n >= BANKS:
                pe.wait_ge(tile_free[n % BANKS], n // BANKS + beyond)

        def full(job, ins):
            ins.then_inc(tile_full[JOB[job] % BANKS], 1)

        def free(job, ins):
            ins.then_inc(tile_free[JOB[job] % BANKS], 1)

        def static_loads(p):
            return (S_MOE - 1 - p) // RING + 1

        def loads_before(l, p):
            return l * (static_loads(p) + TURNS)

        def before(eng, e):
            return eng.value_load(tab[0:1, e:e + 1] if isinstance(e, int) else tab[0:1, bass.ds(e, 1)],
                                  min_val=0, max_val=NEXP + 2 * NTOK // BS)

        def each_block(eng, i, odd, body):
            base = before(eng, i * 2 + odd)
            count = eng.value_load(tab[0:1, bass.ds(i * 2 + (odd + NEXP + 1), 1)], min_val=1, max_val=NTOK // BS)
            with eng.Fori(0, count) as b:
                body(b, base + b)

        def wait_added(eng, l):
            total = before(eng, NEXP)
            for o in range(2):
                eng.wait_ge(add_done[l][o], total * 4 + 5)

        const_dram = const
        units = [attention_units(l) for l in range(LAYERS)]
        n_before = [0, len(units[0])]
        n_lat = [sum(u[0] == 1 and u[3] >= CTX for u in us) for us in units]
        LOADS = 4
        block = ctx.enter_context(nc.Block())

        @block.sync
        def _(sp):
            sp.dma_start(con[:], const_dram).then_inc(const_in, 16)
            sp.dma_start(mis[:], misc.rearrange("l p n -> p l n")).then_inc(const_in, 16)
            sp.dma_start(x[:], xT.rearrange("(k p) n -> p k n", p=P)).then_inc(const_in, 16)
            def load(dst, arrived, n):
                src = wpack[n] if isinstance(n, int) else wpack[bass.ds(n, 1)].rearrange("a p n -> (a p) n")
                sp.dma_start(dst, src).then_inc(arrived, 16)

            for l in range(LAYERS):
                first = l * PER_LAYER
                if l:
                    sp.wait_ge(down_full[l - 1], before(sp, NEXP - 1) * 2)
                for n in range(RING):
                    load(ring[:, n, :], slot_in[n], first + n)
                with sp.Fori(1, S_MOE // RING) as i:
                    for n in range(RING):
                        sp.wait_ge(slot_used, (i - 1) * RING + (l * S_MOE + n + 1))
                        load(ring[:, n, :], slot_in[n], i * RING + (first + n))
                for n in range(S_MOE // RING * RING, S_MOE):
                    sp.wait_ge(slot_used, l * S_MOE + n - RING + 1)
                    load(ring[:, n % RING, :], slot_in[n % RING], first + n)
                for n in range(RING):
                    held = (S_MOE - 1 - n) // RING * RING + n
                    sp.wait_ge(slot_used, l * S_MOE + held + 1)
                    load(ring[:, n, :], slot_in[n], first + S_MOE + n)
                for o in range(2):
                    sp.wait_ge(out_free[o], (l + 1) * KW)
                sp.wait_ge(glu_done, (l + 1) * KW)
                for n in range(RING):
                    load(twin[n], twin_in[n], first + S_MOE + RING + n)
                sp.wait_ge(route_done, l + 1)
                with sp.Fori(1, TURNS) as i:
                    for odd in range(2):
                        sp.wait_ge(down_full[l], before(sp, i * 2 + (odd - 1)) * 2)
                        for n in range(RING):
                            load(twin[n] if odd else ring[:, n, :], (twin_in if odd else slot_in)[n],
                                 i * (2 * RING) + (first + S_MOE + odd * RING + n))
            for m in range(KD):
                sp.wait_ge(fin_done, m + 1)
                sp.dma_start(outT[m * P:(m + 1) * P, :], h[:, m, CTX:]).then_inc(stored, 16)
            sp.wait_ge(stored, 16 * KD)

        @block.tensor
        def _(pe):
            def mm(out, lhsT, rhs, start=True, stop=True):
                return nc.tensor.matmul(out, lhsT, rhs, start=start, stop=stop)

            def slot(l, n, parts=KD):
                pe.wait_ge(slot_in[n % RING], 16 * (loads_before(l, n % RING) + n // RING + 1))
                return ring[:, n % RING, :].rearrange("p (k n) -> p k n", k=parts)

            def product(job, terms, out=None, release=0, begin=True, end=True):
                if begin:
                    wait_bank(pe, job)
                out = bank(job) if out is None else out
                for k, (lhsT, rhs) in enumerate(terms):
                    ins = mm(out, lhsT, rhs, k == 0, k == len(terms) - 1)
                    if k == 0 and release:
                        ins.then_inc(slot_used, release)
                if end:
                    full(job, ins)

            def mean_square(job, nn, c0, release=0):
                wait_bank(pe, job)
                for k in range(KD):
                    pe.wait_ge(sq_done, nn * KD + k + 1)
                    ins = mm(bank(job)[:, c0:], c("model_mean"), h[:, k, c0:], k == 0, k == KD - 1)
                    if k == 0 and release:
                        ins.then_inc(slot_used, release)
                full(job, ins)

            def project(job, w, m, src, c0, release=0):
                product(job, [(w[:, k, m * P:(m + 1) * P], src[:, k, c0:]) for k in range(w.shape[1])],
                        bank(job)[:, c0:], release)

            for l in range(LAYERS):
                c0 = 0 if l == 0 else CTX
                if l == 0:
                    pe.wait_ge(const_in, 48)
                    pe.wait_ge(csil_done, 1)
                job = (l, "mod")
                for n in range(24):
                    w = slot(l, S_MOD + n)
                    for t in range(2):
                        col = 4 * n + 2 * t
                        product(job, [(w[:, k, t * P:(t + 1) * P], csil[:, k, :]) for k in range(KD)],
                                bank(job)[:, col:col + 2], int(t == 0 and n > 0), col == 0, n == 23 and t == 1)
                mean_square((l, "ms1"), 2 * l, 0, 1)

                pe.wait_ge(h_done, (2 * l + 1) * KD)
                for m in range(KW):
                    project((l, "u", m), slot(l, S_U + m // 2), m % 2, h, 0, int(m == 2))
                for q in range(NQ):
                    pe.wait_ge(wm_done, l * NQ + q + 1)
                    for r in range(2):
                        job = (l, "wt", q, r)
                        wait_bank(pe, job)
                        for g in range(GQ):
                            ins = nc.tensor.transpose(bank(job)[:, g * P:(g + 1) * P],
                                                      wm[:, r, g].rearrange("p j h -> p (j h)"), c("ident"))
                        full(job, ins)
                    job = (l, "st", q)
                    wait_bank(pe, job)
                    for r in range(2):
                        wait_taken(pe, (l, "wt", q, r))
                    pe.wait_ge(ug_in, 16 * STEP * (l + 1))
                    for g in range(GQ):
                        for r in range(2):
                            ins = mm(bank(job)[:, (2 * g + r) * NCH:(2 * g + r + 1) * NCH], wt[:, r, g, :],
                                     ug[:, q * GQ + g, :])
                    full(job, ins)
                for m in range(KW):
                    project((l, "qa", m), slot(l, S_QA + m // 2), m % 2, h, c0, 1 - m % 2)
                w = slot(l, S_KV)
                project((l, "ka"), w, 0, h, 0, 1)
                job = (l, "va")
                for t in range(NTOK // P):
                    product(job, [(h[:, k, t * P:(t + 1) * P], w[:, k, P:]) for k in range(KD)],
                            bank(job)[:, t * P:(t + 1) * P], 0, t == 0, t == NTOK // P - 1)
                for m in range(KW):
                    project((l, "qn", m), slot(l, S_QN + m // 2), m % 2, h, c0, 1 - m % 2)
                for m in range(KW):
                    project((l, "kn", m), slot(l, S_KN + m // 2), m % 2, h, 0, 1 - m % 2)
                ws = slot(l, S_VN), slot(l, S_VN + 1)
                for t in range(NTOK // P):
                    job = (l, "vn", t)
                    for n, w in enumerate(ws):
                        product(job, [(h[:, k, t * P:(t + 1) * P], w[:, k, :]) for k in range(KD)],
                                bank(job)[:, n * 256:(n + 1) * 256], int(t + n == 0), n == 0, n == 1)
                for m in range(KW + 1):
                    t = c0 if m < KW else 0
                    pe.wait_ge(qsq_done, l * (KW + 1) + m + 1)
                    product((l, "qk_ms", m), [(c("head_mean"), qsq[:, t:])], bank((l, "qk_ms", m))[:, t:])
                    pe.wait_ge(qnorm_done, l * (KW + 1) + m + 1)
                    v = qa[:, m, CTX:] if m < KW else ka[:, CTX:]
                    product((l, "rope", m), [(c("rot"), v)], bank((l, "rope", m))[:, 0:LAT])
                zw = (NPOS - 2) * GRP
                for q in range(NQ + 1):
                    if q < NQ:
                        pe.wait_ge(cp_done, l * NQ + q + 1)
                        for n in range(2):
                            for g in range(2):
                                gg = 2 * n + g
                                product((l, "z", q, n),
                                        [(bb[:, r, q * GQ + gg, :],
                                          cp[:, r, (q % 2) * GQ + gg, 1:NPOS - 1, :].rearrange("p a b -> p (a b)"))
                                         for r in range(2)],
                                        bank((l, "z", q, n))[0:GRP, g * zw:(g + 1) * zw], 0, g == 0, g == 1)
                    if q:
                        o = q - 1
                        job = (l, "y", o)
                        pe.wait_ge(tm_in, 16 * STEP * (l * NQ + o + 1))
                        pe.wait_ge(scan_done, l + 1)
                        for g in range(GQ):
                            G = o * GQ + g
                            terms = [(tm[:, o % 2, g, :], ug[:, G, :])]
                            for r in range(2):
                                co = cp[:, r, (o % 2) * GQ + g].rearrange("p a b -> p (a b)")
                                terms.append((co[:, (STEP + 1) * GRP:], st[:, r, G, 0:NCH]))
                                s = st[:, r, G, 0:NCH].rearrange("p (a c) -> p a c", a=2)[:, :, ::-1]
                                terms.append((co[:, 0:STEP * GRP], s))
                            product(job, terms, bank(job)[:, g * NCH:(g + 1) * NCH], 0, g == 0, g == GQ - 1)
                us = units[l]
                pe.wait_ge(rope_done, (l + 1) * (KW + 1))
                for t in range(NTOK // P):
                    wait_taken(pe, (l, "vn", t))
                for n in range(len(us) + 3):
                    if n < len(us):
                        br, i, half, q0, nk = us[n]
                        qq, kk = (qa[:, i], ka[:, :]) if br == 0 else (qn[:, i], kn[:, i])
                        a = half * HD
                        product((l, "sc", n), [(qq[a:a + HD, q0:q0 + P], kk[a:a + HD, 0:nk])],
                                bank((l, "sc", n))[:, 0:nk])
                    if 2 <= n < len(us) + 2:
                        N, nk = n_before[l] + n - 2, us[n - 2][4]
                        if N >= 2:
                            pe.wait_ge(turn_free[N % 2], N // 2)
                        pe.wait_ge(prob_done, N + 1)
                        for t in range(nk // P):
                            ins = nc.tensor.transpose(turn_ps[:, N % 2, t * P:(t + 1) * P],
                                                      probs[:, N % 3, t * P:(t + 1) * P], c("ident"))
                        ins.then_inc(turn_full[N % 2], 1)
                    if n >= 3:
                        N, (br, i, half, q0, nk) = n_before[l] + n - 3, us[n - 3]
                        O = (l * 2 + br) * KW + i
                        if (half, q0) == (0, c0) and O >= 2:
                            pe.wait_ge(out_free[O % 2], O // 2)
                        pe.wait_ge(turn_free[N % 2], N // 2 + 1)
                        a = half * HD
                        for t in range(nk // P):
                            v = va[:, t, a:a + HD] if br == 0 else vn[:, t, i * P + a:i * P + a + HD]
                            ins = mm(out_ps[a:a + HD, O % 2, q0:q0 + P], v, pt[:, N % 2, t, :],
                                     t == 0, t == nk // P - 1)
                        if (half, q0) == (1, NTOK - P):
                            ins.then_inc(out_full[O % 2], 1)
                pe.wait_ge(gelu_done, (l + 1) * KW)
                for m in range(KW):
                    project((l, "glu", m), slot(l, S_GLU, KW), m, z, c0, 2 if m == 0 else 0)
                for hf in range(2):
                    for b in range(3):
                        n = S_MIX + (hf * 3 + b) * 3
                        for m in range(KW):
                            w = slot(l, n + (0 if m < 2 else 2))
                            first = hf + b == 0
                            project((l, "gate", hf, b, m), w, m % 2, h, c0,
                                    {0: 1 if first else 2, 2: 1}.get(m, 0))
                            if hf + m == 0:
                                if b == 0:
                                    pe.wait_ge(glu_done, (l + 1) * KW)
                                else:
                                    for O in ((l * 2 + b) * KW - 2, (l * 2 + b) * KW - 1):
                                        pe.wait_ge(out_free[O % 2], O // 2 + 1)
                            project((l, "br", hf, b, m), slot(l, n + 1, KW), m, bo[b], c0)
                pe.wait_ge(mix_done, (l + 1) * 4 * KW)
                for m in range(KD):
                    project((l, "wo", m), slot(l, S_OUT + m // 2), m % 2, mg, c0,
                            {0: 2, 2: 1, 4: 1, 6: 1}.get(m, 0))
                mean_square((l, "ms2"), 2 * l + 1, c0, 1)
                pe.wait_ge(h_done, (2 * l + 2) * KD)
                job = (l, "rt")
                tiles = range(c0 // P, NTOK // P)
                for t in tiles:
                    product(job, [(h[:, k, t * P:(t + 1) * P], c("rw")[:, k * NEXP:(k + 1) * NEXP]) for k in range(KD)],
                            bank(job)[:, t * NEXP:(t + 1) * NEXP], 0, t == tiles[0], t == tiles[-1])
                for t in tiles:
                    for n in range(2):
                        job = (l, "ht", t, n)
                        wait_bank(pe, job)
                        for k in range(4):
                            ins = nc.tensor.transpose(bank(job)[:, k * P:(k + 1) * P],
                                                      h[:, 4 * n + k, t * P:(t + 1) * P], c("ident"))
                        full(job, ins)
                pe.wait_ge(chosen, l + 1)
                pe.wait_ge(late_in, 16 * (l + 1))
                pick = rt[:, R_PICK]
                job = (l, "rank")
                for t in tiles:
                    product(job, [(c("model_mean"), pick[:, s]) for s in tiles if s < t] +
                            [(lat_[:, LATE["before"]], pick[:, t])],
                            bank(job)[:, t * NEXP:(t + 1) * NEXP], 0, t == tiles[0], False)
                product(job, [(c("model_mean"), pick[:, t]) for t in tiles], bank(job)[:, 64:64 + NEXP], 0, False)
                for j in [(l, "rank")] + [(l, "ht", t, n) for t in tiles for n in range(2)]:
                    wait_taken(pe, j)
                pe.wait_ge(route_done, l + 1)

                def turn_outputs(r):
                    for o in range(2):
                        pe.wait_ge(add_done[l][o], r * 4 + 1)
                    pe.wait_ge(yT_done[l], r * 2 + 2)
                    for m in range(KD):
                        ins = nc.tensor.transpose(turn_ps[:, m // 4, (m % 4) * P:(m % 4 + 1) * P], yT[:, m, :],
                                                  c("ident"))
                    ins.then_inc(yt_full[l], 1)

                def add_outputs(r):
                    pe.wait_ge(ys_done[l], r + 1)
                    for m in range(KD):
                        pe.wait_ge(add_done[l][m % 2], r * 4 + (m // 2 + 1))
                        mm(turn_ps[:, m % 2, c0:], ys[:, m * P:(m + 1) * P], sw[:, c0:])\
                            .then_inc(add_full[l][m % 2], 1)

                def block_products(w, b, r):
                    pe.wait_ge(sw_done[l], r + 1)
                    pe.wait_ge(sel_done[l], r + 1)
                    for k in range(KD):
                        for t in tiles:
                            ins = mm(tile_ps[:, k // 4, (k % 4) * BS:(k % 4 + 1) * BS],
                                     ht[:, t, k * P:(k + 1) * P], sel[:, t], t == tiles[0], t == tiles[-1])
                        if k % 4 == 3:
                            ins.then_inc(gather_full[l], 1)
                    turn_outputs(r)
                    pe.wait_ge(hs_done[l], r * 2 + 2)
                    for f in range(2 * KF):
                        wf = w[2 * (f % KF // 2) + f // KF].rearrange("p (k n) -> p k n", k=KD)
                        for k in range(KD):
                            ins = mm(tile_ps[:, 2 + f // KF, (f % KF) * BS:(f % KF + 1) * BS],
                                     wf[:, k, (f % 2) * P:(f % 2 + 1) * P], hs[:, k], k == 0, k == KD - 1)
                        if f % KF == KF - 1:
                            ins.then_inc(gu_full[l], 1)
                    add_outputs(r)
                    for t in tiles:
                        ins = nc.tensor.transpose(tile_ps[:, 0, t * P:(t + 1) * P], selw[:, t], c("ident"))
                    ins.then_inc(w_full[l], 1)
                    pe.wait_ge(hid_done[l], r + 1)
                    for m in range(KD):
                        wd = w[4 + m // 4].rearrange("p (k n) -> p k n", k=KF)
                        for k in range(KF):
                            ins = mm(out_ps[:, m // 4, (m % 4) * BS:(m % 4 + 1) * BS],
                                     wd[:, k, (m % 4) * P:(m % 4 + 1) * P], hid[:, k], k == 0, k == KF - 1)
                        if m % 4 == 3:
                            ins.then_inc(down_full[l], 1)

                with pe.Fori(0, TURNS) as i:
                    for odd in range(2):
                        for n in range(RING):
                            if odd:
                                pe.wait_ge(twin_in[n], i * 16 + 16 * (l * TURNS + 1))
                            else:
                                pe.wait_ge(slot_in[n], i * 16 + 16 * (loads_before(l, n) + static_loads(n) + 1))
                        w = twin if odd else [ring[:, n, :] for n in range(RING)]
                        each_block(pe, i, odd, lambda b, r: block_products(w, b, r))
                total = before(pe, NEXP)
                turn_outputs(total)
                add_outputs(total)
                for o in range(2):
                    pe.wait_ge(add_done[l][o], total * 4 + 5)
            mean_square((LAYERS, "ms"), 2 * LAYERS, CTX)

        @block.scalar
        def _(act):
            A = nc.scalar.activation
            link = Link(act, act_link)

            def copy(job, out, src):
                wait_full(act, job)
                free(job, nc.scalar.copy(out, src))

            def squares(nn, c0, ready):
                for k in range(KD):
                    ready(k)
                    A(h[:, k, c0:], x[:, k, c0:], ACT.Square).then_inc(sq_done, 1)

            def root(nn, job, c0):
                wait_taken(act, job)
                A(rstd[:, c0:], rstd[:, c0:], ACT.Sqrt).then_inc(root_done, 1)

            def modulate(nn, which, c0):
                for k in range(KD):
                    act.wait_ge(hx_done, nn * KD + k + 1)
                    for s in range(c0 // CTX, 2):
                        ins = A(h[:, k, s * CTX:(s + 1) * CTX], h[:, k, s * CTX:(s + 1) * CTX], ACT.Identity,
                                scale=amul[:, which, k, s:s + 1], bias=mod[:, 3 * which, k, s:s + 1])
                    ins.then_inc(h_done, 1)

            act.wait_ge(const_in, 48)
            A(csil[:].rearrange("p a b -> p (a b)"), c("c"), ACT.Silu).then_inc(csil_done, 1)
            for l in range(LAYERS):
                c0 = 0 if l == 0 else CTX
                if l:
                    wait_added(act, l - 1)
                act.dma_start(sm, ssm[l]).then_inc(ssm_in, 16)
                act.dma_start(dsk.rearrange("p a b -> p (a b)"), dskip[l]).then_inc(ssm_in, 16)
                squares(2 * l, 0, lambda k: None)
                act.wait_ge(ssm_in, 32 * (l + 1))
                A(t8[:, 0], s_("ldt"), ACT.Exp).then_inc(trig_out, 1)
                act.wait_ge(trig_in, 2 * l + 1)
                A(t8[:, 1], t8[:, 1], ACT.Exp).then_inc(trig_out, 1)
                act.wait_ge(trig_in, 2 * l + 2)
                A(t8[:, 4], t8[:, 2], ACT.Sin).then_inc(trig_out, 1)
                A(t8[:, 5], t8[:, 2], ACT.Sin, scale=0.5).then_inc(trig_out, 1)
                root(2 * l, (l, "ms1"), 0)
                act.wait_ge(mod_done, l + 1)
                modulate(2 * l, 0, 0)
                for m in range(KW):
                    wait_taken(act, (l, "u", m))
                act.dma_start(u_dram.rearrange("(t p) j c -> p t (j c)", p=P), up).then_inc(u_out, 16)
                act.wait_ge(u_out, 16 * (l + 1))
                for j in range(STEP):
                    act.dma_start(ug[j * GRP:(j + 1) * GRP],
                                  u_dram[:, j, :].rearrange("(g h) c -> h g c", h=GRP)).then_inc(ug_in, 16)
                for q in range(NQ):
                    for r in range(2):
                        job = (l, "wt", q, r)
                        wait_full(act, job)
                        if q:
                            wait_full(act, (l, "st", q - 1))
                        free(job, nc.scalar.copy(wt[:, r].rearrange("p g n -> p (g n)"), bank(job)))
                for m in range(KW):
                    copy((l, "qa", m), qa[:, m, c0:], bank((l, "qa", m))[:, c0:])
                copy((l, "ka"), ka[:], bank((l, "ka")))
                copy((l, "va"), va[:].rearrange("p t n -> p (t n)"), bank((l, "va")))
                for m in range(KW):
                    job = (l, "qn", m)
                    wait_full(act, job)
                    free(job, nc.scalar.mul(qn[:, m, c0:], bank(job)[:, c0:], HD ** -0.5))
                for m in range(KW):
                    copy((l, "kn", m), kn[:, m, :], bank((l, "kn", m)))
                for t in range(NTOK // P):
                    copy((l, "vn", t), vn[:, t, :], bank((l, "vn", t)))
                for m in range(KW + 1):
                    t = c0 if m < KW else 0
                    src = qa[:, m, t:] if m < KW else ka[:, t:]
                    if m == 0:
                        for mm_ in range(KW):
                            wait_taken(act, (l, "qa", mm_))
                        wait_taken(act, (l, "ka"))
                    else:
                        wait_full(act, (l, "qk_ms", m - 1))
                    A(qsq[:, t:], src, ACT.Square).then_inc(qsq_done, 1)
                    wait_taken(act, (l, "qk_ms", m))
                    A(qrs[:, t:], qrs[:, t:], ACT.Sqrt).then_inc(qroot_done, 1)
                for q in range(NQ):
                    if q:
                        act.wait_ge(tm_in, 16 * STEP * (l * NQ + q))
                    for n in range(2):
                        job = (l, "z", q, n)
                        copy(job, zs[:, 2 * n:2 * n + 2].rearrange("p g n -> p (g n)"), bank(job)[0:GRP, 0:480])
                    act.wait_ge(zd_done, l * NQ + q + 1)
                    if q >= 2:
                        wait_full(act, (l, "y", q - 2))
                    for j in range(STEP):
                        a = (STEP - 1 - j) * GRP
                        act.dma_start(tm[j * GRP:(j + 1) * GRP, q % 2], zs[:, :, a:a + P]).then_inc(tm_in, 16)
                    if q:
                        copy((l, "y", q - 1), ug[:, (q - 1) * GQ:q * GQ].rearrange("p g c -> p (g c)"),
                             bank((l, "y", q - 1))[:, 0:GQ * NCH])
                copy((l, "y", NQ - 1), ug[:, (NQ - 1) * GQ:].rearrange("p g c -> p (g c)"),
                     bank((l, "y", NQ - 1))[:, 0:GQ * NCH])
                for q in range(NQ):
                    wait_taken(act, (l, "y", q))
                for j in range(STEP):
                    act.dma_start(y_dram[:, j, :].rearrange("(g h) c -> h g c", h=GRP),
                                  ug[j * GRP:(j + 1) * GRP]).then_inc(y_out, 16)
                act.wait_ge(y_out, 16 * STEP * (l + 1))
                act.dma_start(yt, y_dram.rearrange("(t p) j c -> p t (j c)", p=P)).then_inc(y_in, 16)
                for r in range(GRID_H):
                    for rk in range(GRID_H):
                        row = l * HEADS * RPB_ROWS + RPB_ROWS // 2 + rk - r
                        act.dma_start(
                            bias[(r % 2) * GRID_W:(r % 2 + 1) * GRID_W, r // 2, :, rk],
                            bass.AP(tensor=rpb.tensor, offset=row * GRID_W * RPB_PAD + GRID_W - 1,
                                    ap=[[RPB_PAD - 1, GRID_W], [RPB_ROWS * GRID_W * RPB_PAD, HEADS], [1, GRID_W]]))\
                            .then_inc(bias_in, 16)
                us = units[l]
                for n in range(len(us) + 4):
                    if n < len(us):
                        N, nk = n_before[l] + n, us[n][4]
                        act.wait_ge(max_done, N + 1)
                        if N >= 3:
                            act.wait_ge(turn_full[(N - 3) % 2], (N - 3) // 2 + 1)
                        free((l, "sc", n),
                             A(probs[:, N % 3, 0:nk], bank((l, "sc", n))[:, 0:nk], ACT.Exp,
                               bias=smx[:, 0, N % 64:N % 64 + 1], accum_out=smx[:, 1, N % 64:N % 64 + 1]))
                    if n >= 4 and us[n - 4][2:4] == (1, NTOK - P):
                        br, i = us[n - 4][0:2]
                        O = (l * 2 + br) * KW + i
                        act.wait_ge(out_full[O % 2], O // 2 + 1)
                        nc.scalar.copy(bo[1 + br][:, i, c0:], out_ps[:, O % 2, c0:]).then_inc(out_free[O % 2], 1)
                act.wait_ge(y_in, 16 * (l + 1))
                for t in range(KW):
                    src = yt[:, t].rearrange("p (j c) -> p c j", j=STEP)[:, c0 // STEP:, :]
                    A(z[:, t, c0:].rearrange("p (c j) -> p c j", j=STEP), src, ACT.Gelu_apprx_tanh)\
                        .then_inc(gelu_done, 1)
                act.wait_ge(gelu_done, (l + 1) * KW)
                act.dma_start(lat_, late).then_inc(late_in, 16)
                for m in range(KW):
                    if m >= 2:
                        act.wait_ge(glu_done, l * KW + m - 1)
                    job = (l, "glu", m)
                    wait_full(act, job)
                    free(job, A(sig[:, m % 2, c0:], bank(job)[:, c0:], ACT.Sigmoid))
                act.wait_ge(glu_done, (l + 1) * KW)
                order = [(l, "br", hf, b, m) for hf in range(2) for b in range(3) for m in range(KW)]
                for n, (_, _, hf, b, m) in enumerate(order):
                    if n >= 2:
                        wait_taken(act, order[n - 2])
                    job = (l, "gate", hf, b, m)
                    wait_full(act, job)
                    free(job, A(sig[:, n % 2, c0:], bank(job)[:, c0:], ACT.Sigmoid))
                squares(2 * l + 1, c0, lambda k: wait_taken(act, (l, "wo", k)))
                root(2 * l + 1, (l, "ms2"), c0)
                modulate(2 * l + 1, 1, c0)
                act.wait_ge(rl_done, l + 1)
                A(rt[:, 3, c0 // P:], rt[:, 2, c0 // P:], ACT.Exp).then_inc(re_done, 1)
                for t in range(c0 // P, NTOK // P):
                    for n in range(2):
                        copy((l, "ht", t, n), ht[:, t, n * 512:(n + 1) * 512], bank((l, "ht", t, n)))

                def copy_outputs(r):
                    act.wait_ge(yt_full[l], r + 1)
                    nc.scalar.copy(ys.rearrange("p (a n) -> p a n", a=2), turn_ps[:]).then_inc(ys_done[l], 1)

                def block_copies(b, r):
                    for n in range(2):
                        act.wait_ge(gather_full[l], r * 2 + (n + 1))
                        nc.scalar.copy(hs[:, 4 * n:4 * n + 4].rearrange("p k n -> p (k n)"), tile_ps[:, n, :])\
                            .then_inc(hs_done[l], 1)
                    copy_outputs(r)
                    act.wait_ge(gu_full[l], r * 2 + 1)
                    A(sg.rearrange("p k n -> p (k n)"), tile_ps[:, 2, :], ACT.Silu).then_inc(sg_done[l], 1)
                    act.wait_ge(w_full[l], r + 2)
                    nc.scalar.copy(sw[:, c0:], tile_ps[:, 0, c0:]).then_inc(sw_done[l], 1)
                    for n in range(2):
                        act.wait_ge(down_full[l], r * 2 + (n + 1))
                        nc.scalar.copy(yT[:, 4 * n:4 * n + 4].rearrange("p k n -> p (k n)"), out_ps[:, n, :])\
                            .then_inc(yT_done[l], 1)

                act.wait_ge(route_done, l + 1)
                with act.Fori(0, TURNS) as i:
                    for odd in range(2):
                        each_block(act, i, odd, block_copies)
                copy_outputs(before(act, NEXP))
            wait_added(act, LAYERS - 1)
            squares(2 * LAYERS, CTX, lambda k: None)
            root(2 * LAYERS, (LAYERS, "ms"), CTX)

        def into_steps(dve, link, l, q):
            job = (l, "st", q)
            gs = slice(q * GQ, (q + 1) * GQ)
            v = bank(job).rearrange("p (g r c) -> p r g c", r=2, c=NCH)
            wait_full(dve, job)
            dve.tensor_copy(st[0:NST, :, gs, 1:], v[0:NST])
            dve.tensor_copy(st[NST:P, :, gs, 1:NCC + 1][:, :, :, ::-1], v[NST:P, :, :, 0:NCC])
            free(job, dve.tensor_copy(st[NST:P, :, gs, NCC + 1:][:, :, :, ::-1], v[NST:P, :, :, NCC:]))

        @block.vector
        def _(dve):
            link = Link(dve, dve_link)
            TT, TS, STT, CP = dve.tensor_tensor, dve.tensor_scalar, dve.scalar_tensor_tensor, dve.tensor_copy

            def discretise(l):
                lre, lim = s_("lre"), s_("lim")
                dt, er, th, n = (t8[:, k] for k in range(4))
                dve.wait_ge(ssm_in, 32 * (l + 1))
                dve.wait_ge(trig_out, 4 * l + 1)
                TT(er, lre, dt, ALU.mult).then_inc(trig_in, 1)
                link(TT(th, lim, dt, ALU.mult))
                link(TS(n, th, 1 / (2 * math.pi), ROUND, ALU.mult, ALU.add))
                link(TS(n, n, ROUND, None, ALU.subtract))
                for part in (TWO_PI_1, TWO_PI_2, TWO_PI_3):
                    link(STT(th, n, -part, th, ALU.mult, ALU.add))
                TS(th, th, PI_BELOW, -PI_BELOW, ALU.min, ALU.max).then_inc(trig_in, 1)
                link(dve.memset(pw[:, 0, 0], 1.0))
                link(dve.memset(pw[:, 1, 0], 0.0))
                link(dve.memset(pws, 0.0))
                link(dve.memset(st[:, :, :, 0], 0.0))
                dve.wait_ge(trig_out, 4 * l + 4)
                sn, sh, cs = t8[:, 4], t8[:, 5], t8[:, 6]
                link(TT(cs, sh, sh, ALU.mult))
                link(TS(cs, cs, -2.0, 1.0, ALU.mult, ALU.add))
                ar, ai = pw[:, 0, 1], pw[:, 1, 1]
                link(TT(ar, er, cs, ALU.mult))
                link(TT(ai, er, sn, ALU.mult))
                inv, am, nr, ni, tmp = (t8[:, k] for k in range(7, 12))
                link(TT(inv, lre, lre, ALU.mult))
                link(TT(tmp, lim, lim, ALU.mult))
                link(TT(inv, inv, tmp, ALU.add))
                link(dve.reciprocal(inv, inv))
                link(TS(am, ar, 1.0, None, ALU.subtract))
                link(TT(nr, am, lre, ALU.mult))
                link(TT(tmp, ai, lim, ALU.mult))
                link(TT(nr, nr, tmp, ALU.add))
                link(TT(nr, nr, inv, ALU.mult))
                link(TT(ni, ai, lre, ALU.mult))
                link(TT(tmp, am, lim, ALU.mult))
                link(TT(ni, ni, tmp, ALU.subtract))
                link(TT(ni, ni, inv, ALU.mult))
                bre, bim = (s_(k).rearrange("p (g h) -> p g h", h=GRP) for k in ("bre", "bim"))
                nrb, nib = spread(nr, 2, GRP), spread(ni, 2, GRP)
                tb = wtmp.rearrange("p a b c -> p (a b c)")[:, 0:NGRP * GRP].rearrange("p (g h) -> p g h", h=GRP)
                link(TT(bb[:, 0], bre, nrb, ALU.mult))
                link(TT(tb, bim, nib, ALU.mult))
                link(TT(bb[:, 0], bb[:, 0], tb, ALU.subtract))
                link(TT(bb[:, 1], bim, nrb, ALU.mult))
                link(TT(tb, bre, nib, ALU.mult))
                link(TT(bb[:, 1], bb[:, 1], tb, ALU.add))
                for n in (1, 2, 4):
                    lo, hi = slice(1, n + 1), slice(n + 1, 2 * n + 1)
                    fr, fi = spread(pw[:, 0, n], 1, n), spread(pw[:, 1, n], 1, n)
                    tp = sst.rearrange("p a b g -> p (a b) g")[:, 0:n]
                    link(TT(pw[:, 0, hi], pw[:, 0, lo], fr, ALU.mult))
                    link(TT(tp, pw[:, 1, lo], fi, ALU.mult))
                    link(TT(pw[:, 0, hi], pw[:, 0, hi], tp, ALU.subtract))
                    link(TT(pw[:, 1, hi], pw[:, 0, lo], fi, ALU.mult))
                    link(TT(tp, pw[:, 1, lo], fr, ALU.mult))
                    link(TT(pw[:, 1, hi], pw[:, 1, hi], tp, ALU.add))
                F, B = slice(0, NST), slice(NST, P)
                link(CP(pww[F], pw[F, :, 0:STEP][:, :, ::-1]))
                link(CP(pww[B], pw[B, :, 0:STEP]))
                for d, at in ((F, slice(STEP, NPOS)), (B, slice(0, STEP + 1))):
                    for r, sign in ((0, 1.0), (1, -1.0)):
                        src = pw[d, r] if d is F else pw[d, r][:, ::-1]
                        link(TS(pws[d, r, at], src, sign, None, ALU.mult))
                a8r, a8i = pw[:, 0, STEP], pw[:, 1, STEP]
                link(CP(a8s[:, 0], spread(a8r, 1, 2)))
                link(TS(a8s[:, 1, 0], a8i, -1.0, None, ALU.mult))
                CP(a8s[:, 1, 1], a8i).then_inc(pow_done, 1)
                dve.wait_ge(pow_done, l + 1)

            def rms(nn, job, c0):
                wait_full(dve, job)
                free(job, TS(rstd[:, c0:], bank(job)[:, c0:], EPS, None, ALU.add))
                dve.wait_ge(root_done, nn + 1)
                link(dve.reciprocal(rstd[:, c0:], rstd[:, c0:]))

            def normalise(nn, c0):
                for k in range(KD):
                    TT(h[:, k, c0:], x[:, k, c0:], rstd[:, c0:], ALU.mult).then_inc(hx_done, 1)

            def route(l, c0):
                t0 = c0 // P
                T = NTOK // P - t0
                R = lambda k, n=NEXP: rt[:, k, t0:, 0:n]
                col = lambda k: rt[:, k, t0:, 0:1]

                def wide(v, n):
                    return v.broadcast_to([P, T, n])

                def first_max(out, src, n, m, tmp):
                    link(dve.tensor_reduce(col(m), src, AX.X, ALU.max))
                    link(TT(R(tmp, n), src, wide(col(m), n), ALU.is_equal))
                    iota = spread(c("iota")[:, 0:n], 1, T)
                    link(STT(R(tmp, n), R(tmp, n), -64.0, iota, ALU.mult, ALU.add))
                    link(dve.tensor_reduce(col(m), R(tmp, n), AX.X, ALU.min))
                    link(TT(out, R(tmp, n), wide(col(m), n), ALU.is_equal))

                job = (l, "rt")
                wait_full(dve, job)
                free(job, CP(R(0), bank(job)[:, t0 * NEXP:(NTOK // P) * NEXP].rearrange("p (t e) -> p t e", e=NEXP)))
                wait_taken(dve, job)
                link(dve.tensor_reduce(col(1), R(0), AX.X, ALU.max))
                TT(R(2), R(0), wide(col(1), NEXP), ALU.subtract).then_inc(rl_done, 1)
                dve.wait_ge(re_done, l + 1)
                link(dve.tensor_reduce(col(4), R(3), AX.X, ALU.add))
                link(dve.reciprocal(col(5), col(4)))
                link(TT(R(6), R(3), wide(col(5), NEXP), ALU.mult))
                link(TT(R(7), R(6), spread(c("rb"), 1, T), ALU.add))
                s4 = R(7).rearrange("p t (g e) -> p t g e", e=EGRP)
                one = lambda e: s4[:, :, :, e]
                Q = lambda k: R(k, EGRP)
                link(TT(Q(8), one(0), one(1), ALU.max))
                link(TT(Q(9), one(0), one(1), ALU.min))
                link(TT(Q(10), one(2), one(3), ALU.max))
                link(TT(Q(11), one(2), one(3), ALU.min))
                link(TT(Q(12), Q(8), Q(10), ALU.max))
                link(TT(Q(13), Q(8), Q(10), ALU.min))
                link(TT(Q(14), Q(9), Q(11), ALU.max))
                link(TT(Q(13), Q(13), Q(14), ALU.max))
                link(TT(Q(15), Q(12), Q(13), ALU.add))
                first_max(Q(16), Q(15), EGRP, 17, 18)
                in_g = spread(Q(16), 3, EGRP)
                r19 = R(19).rearrange("p t (g e) -> p t g e", e=EGRP)
                r20 = R(20).rearrange("p t (g e) -> p t g e", e=EGRP)
                link(TS(r19, in_g, FAR, FAR, ALU.mult, ALU.subtract))
                link(TT(r20, s4, in_g, ALU.mult))
                link(TT(R(20), R(20), R(19), ALU.add))
                first_max(R(21), R(20), NEXP, 17, 18)
                link(STT(R(20), R(21), -3 * FAR, R(20), ALU.mult, ALU.add))
                first_max(R(22), R(20), NEXP, 17, 18)
                TT(R(R_PICK), R(21), R(22), ALU.add).then_inc(chosen, 1)
                dve.wait_ge(chosen, l + 1)
                link(TT(R(6), R(6), R(R_PICK), ALU.mult))
                link(dve.tensor_reduce(col(4), R(6), AX.X, ALU.add))
                link(dve.reciprocal(col(5), col(4)))
                link(TT(R(R_SHARE), R(6), wide(col(5), NEXP), ALU.mult))
                job = (l, "rank")
                wait_full(dve, job)
                link(TS(R(R_SLOT), bank(job)[:, t0 * NEXP:(NTOK // P) * NEXP].rearrange("p (t e) -> p t e", e=NEXP),
                        float(D), 1000.0, ALU.mult, ALU.add))
                n_blk, total = rt[:, 1, 0, :], rt[:, 2, 0, :]
                link(TS(n_blk, bank(job)[:, 64:64 + NEXP], D / BS, (BS - 1) / (2 * BS), ALU.mult, ALU.add))
                free(job, TS(n_blk, n_blk, ROUND, None, ALU.add))
                wait_taken(dve, job)
                link(TS(n_blk, n_blk, ROUND, 1.0, ALU.subtract, ALU.max))
                link(TT(R(R_SLOT), R(R_SLOT), R(R_PICK), ALU.mult))
                link(TS(R(R_SLOT), R(R_SLOT), 1000.0, None, ALU.subtract))
                ones = rt[:, 3, 0, :]
                link(dve.memset(ones, 1.0))
                link(dve.tensor_tensor_scan(total, ones, n_blk, 0.0, ALU.mult, ALU.add))
                link(dve.memset(tab[:, 0:1], 0))
                link(CP(tab[:, 1:NEXP + 1], total))
                link(CP(tab[:, NEXP + 1:], n_blk))
                for n in range(2):
                    dve.memset(yT[:, 4 * n:4 * n + 4], 0.0).then_inc(yT_done[l], 1)
                dve.memset(sw, 0.0).then_inc(sw_done[l], 1)
                dve.memset(sel[:, 0], 0.0).then_inc(w_full[l], 1)
                dve.memset(sel[:, 1], 0.0).then_inc(add_done[l][0], 1)
                dve.memset(sel[:, 2], 0.0).then_inc(add_done[l][1], 1)
                dve.memset(sel[:, 3], 0.0).then_inc(route_done, 1)
                dve.wait_ge(route_done, l + 1)

            dve.wait_ge(const_in, 48)
            for l in range(LAYERS):
                c0 = 0 if l == 0 else CTX
                segs = range(c0 // CTX, 2)
                ms = lambda k: mis[:, l, MISC[k]]
                discretise(l)
                job = (l, "mod")
                wait_full(dve, job)
                free(job, TT(mod[:].rearrange("p a k s -> p (a k) s"), bank(job)[:, 0:96].rearrange("p (a s) -> p a s", s=2),
                             spread(ms("bmod"), 2, 2), ALU.add))
                wait_taken(dve, job)
                link(STT(amul[:, 0], mod[:, 1], 1.0, spread(ms("n1"), 2, 2), ALU.add, ALU.mult))
                link(STT(amul[:, 1], mod[:, 4], 1.0, spread(ms("n2"), 2, 2), ALU.add, ALU.mult))
                TS(qg8[:], ms("qg"), HD ** -0.5, None, ALU.mult).then_inc(mod_done, 1)
                dve.wait_ge(mod_done, l + 1)
                rms(2 * l, (l, "ms1"), 0)
                normalise(2 * l, 0)
                for m in range(KW):
                    job = (l, "u", m)
                    wait_full(dve, job)
                    free(job, CP(up[:, m].rearrange("p (j c) -> p j c", j=STEP),
                                 bank(job).rearrange("p (c j) -> p j c", j=STEP)))
                for q in range(NQ):
                    gs = slice(q * GQ, (q + 1) * GQ)
                    if q:
                        wait_full(dve, (l, "wt", q - 1, 1))
                    pv = [spread(pww[:, r, :, gs].rearrange("p j g -> p g j"), 3, GRP) for r in range(2)]
                    bv = [spread(bb[:, r, gs, :], 2, STEP) for r in range(2)]
                    link(TT(wm[:, 0], pv[0], bv[0], ALU.mult))
                    link(TT(wtmp, pv[1], bv[1], ALU.mult))
                    link(TT(wm[:, 0], wm[:, 0], wtmp, ALU.subtract))
                    link(TT(wm[:, 1], pv[0], bv[1], ALU.mult))
                    link(TT(wtmp, pv[1], bv[0], ALU.mult))
                    TT(wm[:, 1], wm[:, 1], wtmp, ALU.add).then_inc(wm_done, 1)
                    if q:
                        into_steps(dve, link, l, q - 1)
                into_steps(dve, link, l, NQ - 1)
                wait_taken(dve, (l, "st", NQ - 1))
                with dve.Fori(0, NCH) as i:
                    now = st[:, :, :, bass.ds(i, 1)].rearrange("p r g s -> p r (g s)")
                    nxt = st[:, :, :, bass.ds(i + 1, 1)].rearrange("p r g s -> p r (g s)")
                    if l:
                        dve.wait_ge(scan_done, i + l * NCH)
                    TT(sst[:, 0], now, a8s[:, 0], ALU.mult)
                    TT(sst[:, 1, 0], now[:, 1], a8s[:, 1, 0], ALU.mult)
                    link(TT(sst[:, 1, 1], now[:, 0], a8s[:, 1, 1], ALU.mult), i * 2)
                    link(TT(nxt, nxt, sst[:, 0], ALU.add), i * 2)
                    TT(nxt, nxt, sst[:, 1], ALU.add).then_inc(scan_done, 1)
                    dve.wait_ge(scan_done, i + (l * NCH + 1))
                link.n += 2 * (NCH - 1)
                for m in range(KW + 1):
                    t = c0 if m < KW else 0
                    v, g = (qa[:, m], qg8[:, 0:1]) if m < KW else (ka[:, :], ms("kg"))
                    n = l * (KW + 1) + m + 1
                    job = (l, "qk_ms", m)
                    wait_full(dve, job)
                    free(job, TS(qrs[:, t:], bank(job)[:, t:], EPS, None, ALU.add))
                    dve.wait_ge(qroot_done, n)
                    link(dve.reciprocal(qrs[:, t:], qrs[:, t:]))
                    STT(v[:, t:], v[:, t:], g, qrs[:, t:], ALU.mult, ALU.mult).then_inc(qnorm_done, 1)
                    dve.wait_ge(qnorm_done, n)
                    job = (l, "rope", m)
                    wait_full(dve, job)
                    free(job, TT(qrt[:], bank(job)[:, 0:LAT], c("sin"), ALU.mult))
                    link(TT(v[:, CTX:], v[:, CTX:], c("cos"), ALU.mult))
                    wait_taken(dve, job)
                    TT(v[:, CTX:], v[:, CTX:], qrt[:], ALU.add).then_inc(rope_done, 1)
                for q in range(NQ):
                    for n in range(2):
                        wait_taken(dve, (l, "z", q, n))
                    mid = slice((STEP - 1) * GRP, STEP * GRP)
                    TT(zs[:, :, mid], zs[:, :, mid], dsk[:, q * GQ:(q + 1) * GQ, :], ALU.add).then_inc(zd_done, 1)
                us = units[l]
                for n in range(len(us) + 3):
                    if n < len(us):
                        br, i, half, q0, nk = us[n]
                        job = (l, "sc", n)
                        wait_full(dve, job)
                        if br == 1 and q0 >= CTX:
                            dve.wait_ge(bias_done, 2 * (l + 1))
                            v = bank(job)[:, CTX:NTOK]
                            b = bias[:, (q0 - CTX) // P, 2 * i + half].rearrange("p r c -> p (r c)")
                            link(TT(v, v, b, ALU.add))
                        N = n_before[l] + n
                        dve.tensor_reduce(smx[:, 0, N % 64:N % 64 + 1], bank(job)[:, 0:nk], AX.X, ALU.max,
                                          negate=True).then_inc(max_done, 1)
                    if 1 <= n <= len(us):
                        N = n_before[l] + n - 1
                        wait_taken(dve, (l, "sc", n - 1))
                        dve.reciprocal(smx[:, 2, N % 64:N % 64 + 1], smx[:, 1, N % 64:N % 64 + 1]).then_inc(inv_done, 1)
                    if n >= 3:
                        N, nk = n_before[l] + n - 3, us[n - 3][4]
                        dve.wait_ge(turn_full[N % 2], N // 2 + 1)
                        CP(pt[:, N % 2, 0:nk // P].rearrange("p t n -> p (t n)"), turn_ps[:, N % 2, 0:nk])\
                            .then_inc(turn_free[N % 2], 1)
                dve.wait_ge(gelu_done, (l + 1) * KW)
                for m in range(KW):
                    wait_taken(dve, (l, "glu", m))
                    TT(bo[0][:, m, c0:], z[:, m, c0:], sig[:, m % 2, c0:], ALU.mult).then_inc(glu_done, 1)
                mixed = 4 * KW * l
                for n, (hf, b, m) in enumerate((hf, b, m) for hf in range(2) for b in range(3) for m in range(KW)):
                    job = (l, "br", hf, b, m)
                    wait_taken(dve, (l, "gate", hf, b, m))
                    wait_full(dve, job)
                    s, out = sig[:, n % 2, c0:], mg[:, hf * KW + m, c0:]
                    if b == 0:
                        free(job, TT(out, bank(job)[:, c0:], s, ALU.mult))
                    else:
                        v = prod[:, mixed % 2, c0:]
                        if mixed >= 2:
                            dve.wait_ge(mix_done, mixed - 1)
                        free(job, TT(v, bank(job)[:, c0:], s, ALU.mult))
                        wait_taken(dve, job)
                        if b == 1:
                            wait_taken(dve, (l, "br", hf, 0, m))
                        else:
                            dve.wait_ge(mix_done, mixed - KW + 1)
                        TT(out, out, v, ALU.add).then_inc(mix_done, 1)
                        mixed += 1
                for m in range(KD):
                    job = (l, "wo", m)
                    wait_full(dve, job)
                    for s in segs:
                        t = slice(s * CTX, (s + 1) * CTX)
                        ins = STT(x[:, m, t], bank(job)[:, t], mod[:, 2, m, s:s + 1], x[:, m, t], ALU.mult, ALU.add)
                    free(job, ins)
                for m in range(KD):
                    wait_taken(dve, (l, "wo", m))
                rms(2 * l + 1, (l, "ms2"), c0)
                normalise(2 * l + 1, c0)
                route(l, c0)
                T = (NTOK - c0) // P
                S = lambda v: v[:, c0 // P:]

                def add_outputs(r):
                    for m in range(KD):
                        dve.wait_ge(add_full[l][m % 2], r * 4 + (m // 2 + 1))
                        for s in segs:
                            t = slice(s * CTX, (s + 1) * CTX)
                            ins = STT(x[:, m, t], turn_ps[:, m % 2, t], mod[:, 5, m, s:s + 1], x[:, m, t],
                                      ALU.mult, ALU.add)
                        ins.then_inc(add_done[l][m % 2], 1)

                def block_steps(e, b, r):
                    one = lambda k: rt[:, k, c0 // P:, bass.ds(e, 1)].broadcast_to([P, T, BS])
                    slots = spread(lat_[:, bass.ds(b * BS + LATE["slots"].start, BS)], 1, T)
                    dve.wait_ge(w_full[l], r + 1)
                    TT(S(sel), slots, one(R_SLOT), ALU.is_equal).then_inc(eq_done[l], 1)
                    dve.wait_ge(eq_done[l], r + 1)
                    TT(S(selw), S(sel), one(R_SHARE), ALU.mult).then_inc(sel_done[l], 1)
                    dve.wait_ge(sg_done[l], r + 1)
                    dve.wait_ge(gu_full[l], r * 2 + 2)
                    TT(hid.rearrange("p k n -> p (k n)"), tile_ps[:, 3, :],
                       sg.rearrange("p k n -> p (k n)"), ALU.mult).then_inc(hid_done[l], 1)
                    add_outputs(r)

                with dve.Fori(0, TURNS) as i:
                    for odd in range(2):
                        e = i * 2 + odd
                        each_block(dve, i, odd, lambda b, r: block_steps(e, b, r))
                add_outputs(before(dve, NEXP))
                wait_added(dve, l)
            rms(2 * LAYERS, (LAYERS, "ms"), CTX)
            for k in range(KD):
                STT(h[:, k, CTX:], x[:, k, CTX:], c("fg")[:, k:k + 1], rstd[:, CTX:], ALU.mult, ALU.mult)\
                    .then_inc(fin_done, 1)

        @block.gpsimd
        def _(pool):
            link = Link(pool, pool_link)
            TT = pool.tensor_tensor
            pool.wait_ge(const_in, 48)
            for l in range(LAYERS):
                pool.wait_ge(pow_done, l + 1)
                wait_full(pool, (l, "st", NQ - 1))
                wait_full(pool, (l, "wt", NQ - 1, 1))
                cre, cim = (s_(k).rearrange("p (g h) -> p g h", h=GRP) for k in ("cre", "cim"))
                for q in range(NQ):
                    gs = slice(q * GQ, (q + 1) * GQ)
                    if q >= 2:
                        wait_full(pool, (l, "y", q - 2))
                    pv = [spread(pws[:, r, :, gs].rearrange("p n g -> p g n"), 3, GRP) for r in range(2)]
                    cv = [spread(v[:, gs], 2, NPOS) for v in (cre, cim)]
                    o0, o1 = (cp[:, r, (q % 2) * GQ:(q % 2 + 1) * GQ] for r in range(2))
                    link(TT(o0, pv[0], cv[0], ALU.mult))
                    link(TT(ctmp, pv[1], cv[1], ALU.mult))
                    link(TT(o0, o0, ctmp, ALU.add))
                    link(TT(o1, pv[1], cv[0], ALU.mult))
                    link(TT(ctmp, pv[0], cv[1], ALU.mult))
                    TT(o1, o1, ctmp, ALU.subtract).then_inc(cp_done, 1)
                    pool.wait_ge(cp_done, l * NQ + q + 1)
                us = units[l]
                for n in range(len(us)):
                    if n == len(us) // 4:
                        pool.wait_ge(bias_in, 16 * GRID_H ** 2 * (l + 1))
                        for qt in range(2):
                            b = bias[:, qt].rearrange("p h r c -> p (h r) c")
                            TT(b, b, spread(c("far_cols"), 1, HEADS * GRID_H), ALU.add).then_inc(bias_done, 1)
                    N, nk = n_before[l] + n, us[n][4]
                    pool.wait_ge(inv_done, N + 1)
                    v = probs[:, N % 3, 0:nk]
                    pool.tensor_scalar(v, v, smx[:, 2, N % 64:N % 64 + 1], None, ALU.mult).then_inc(prob_done, 1)


def constants(c, c_ctx, router_w, router_b, final_norm_g):
    out = np.zeros((P, N_CON), np.float32)
    out[:, CON["ident"]] = np.eye(P)
    out[:, CON["head_mean"]] = np.kron(np.eye(P // HD), np.full((HD, HD), 1 / HD))
    out[:, CON["model_mean"]] = 1 / D
    n_freq = HD // 4
    rot = np.zeros((P, P), np.float32)
    for a in range(0, P, 2 * n_freq):
        for f in range(n_freq):
            rot[a + n_freq + f, a + f] = -1
            rot[a + f, a + n_freq + f] = 1
    out[:, CON["rot"]] = rot
    t = np.arange(LAT)
    inv = np.float32(10000.0) ** (-np.arange(n_freq, dtype=np.float32) / np.float32(n_freq))
    ang = np.stack([(t // GRID_W).astype(np.float32)[:, None] * inv, (t % GRID_W).astype(np.float32)[:, None] * inv])
    by_channel = np.tile(np.repeat(ang[:, :, None, :], 2, 2).transpose(0, 2, 3, 1).reshape(HD, LAT), (2, 1))
    out[:, CON["cos"]], out[:, CON["sin"]] = np.cos(by_channel), np.sin(by_channel)
    out[:, CON["iota"]] = np.arange(NEXP)
    cq = np.arange(P)[:, None] % GRID_W
    ck = np.arange(GRID_W)[None]
    first = np.clip(cq - WIN_W // 2, 0, GRID_W - WIN_W)
    out[:, CON["far_cols"]] = np.where((ck >= first) & (ck < first + WIN_W), 0, -FAR)
    out[:, CON["rw"]] = router_w.reshape(KD, P, NEXP).transpose(1, 0, 2).reshape(P, -1)
    out[:, CON["rb"]] = router_b
    out[:, CON["fg"]] = final_norm_g.reshape(KD, P).T
    out[:, CON["c"]] = np.stack([c_ctx, c[0]], -1).reshape(KD, P, 2).transpose(1, 0, 2).reshape(P, -1)
    return out


def pack_weights(w_mod, w_in, ssm_w_glu, w_branch, w_out, moe_w_gate, moe_w_up, moe_w_down):
    def by_col(w):
        n = w.shape[1] // 256
        return w.reshape(KD, P, n, 256).transpose(2, 1, 0, 3).reshape(n, P, SLOT)

    def by_half(w):
        n = w.shape[1] // 512
        return w.reshape(KW, P, n, 512).transpose(2, 1, 0, 3).reshape(n, P, SLOT)

    pair = np.arange(WID).reshape(2, KW, HD).transpose(1, 0, 2).reshape(-1)
    slots = []
    for l in range(LAYERS):
        w = w_in[l]
        slots += [by_col(w_mod[l]), by_col(w[:, 0:512]), by_col(w[:, 512:1024][:, pair]),
                  by_col(w[:, 1024:2816])]
        slots.append(by_half(ssm_w_glu[l]))
        gates = [by_col(w[:, 2816 + b * D:2816 + (b + 1) * D]) for b in range(3)]
        branch = [by_half(w_branch[l, 0]), by_half(w_branch[l, 1][pair]), by_half(w_branch[l, 2])]
        for hf in range(2):
            for b in range(3):
                slots += [gates[b][2 * hf:2 * hf + 1], branch[b][hf:hf + 1], gates[b][2 * hf + 1:2 * hf + 2]]
        slots.append(by_col(w_out[l]))
        for e in range(NEXP):
            g, u, d = by_col(moe_w_gate[l, e]), by_col(moe_w_up[l, e]), by_half(moe_w_down[l, e])
            slots += [g[0:1], u[0:1], g[1:2], u[1:2], d]
    return np.concatenate(slots)


def kernel(x, c, ctx, c_ctx, w_mod, b_mod, norm1_g, norm2_g, w_in,
           ssm_lam_re, ssm_lam_im, ssm_log_dt, ssm_b_re, ssm_b_im, ssm_c_re, ssm_c_im,
           ssm_d, ssm_w_glu, gqa_q_norm_g, gqa_k_norm_g, na_rpb, w_branch, w_out,
           router_w, router_b, moe_w_gate, moe_w_up, moe_w_down, final_norm_g):
    import concourse.bacc as bacc
    from concourse.bass_utils import run_bass_kernel_spmd

    f32 = np.float32
    lay = {}
    lay["xT"] = np.concatenate([ctx[0], x[0]]).T
    lay["wpack"] = pack_weights(*(np.asarray(w) for w in (w_mod, w_in, ssm_w_glu, w_branch, w_out,
                                                           moe_w_gate, moe_w_up, moe_w_down)))
    tiles = lambda v: np.asarray(v).reshape(LAYERS, -1, P).transpose(0, 2, 1)
    twice = lambda v: np.tile(np.asarray(v), (1, P // HD))[:, :, None]
    lay["misc"] = np.concatenate([tiles(b_mod), tiles(norm1_g), tiles(norm2_g), twice(gqa_q_norm_g),
                                  twice(gqa_k_norm_g)], 2)
    state = lambda v: np.asarray(v).transpose(0, 1, 3, 2).reshape(LAYERS, P, NGRP)
    ldt = np.repeat(np.asarray(ssm_log_dt)[:, :, None, :], NST, 2).reshape(LAYERS, P, NGRP)
    b_lay = lambda v: np.asarray(v).transpose(0, 1, 3, 2, 4).reshape(LAYERS, P, NGRP * GRP)
    c_lay = lambda v: np.asarray(v).transpose(0, 1, 4, 2, 3).reshape(LAYERS, P, NGRP * GRP)
    lay["ssm"] = np.concatenate([state(ssm_lam_re), state(ssm_lam_im), ldt, b_lay(ssm_b_re), b_lay(ssm_b_im),
                                 c_lay(ssm_c_re), c_lay(ssm_c_im)], 2)
    dskip = np.zeros((LAYERS, GRP, NGRP, GRP), f32)
    for i in range(GRP):
        dskip[:, i, :, i] = np.asarray(ssm_d).reshape(LAYERS, NGRP, GRP)[:, :, i]
    lay["dskip"] = dskip.reshape(LAYERS, GRP, NGRP * GRP)
    rpb = np.zeros((LAYERS, HEADS, RPB_ROWS, RPB_PAD), f32)
    side = (RPB_PAD - RPB_COLS) // 2
    rpb[..., side:side + RPB_COLS] = na_rpb
    lay["rpb"] = np.repeat(rpb[:, :, :, None, :], GRID_W, 3)
    lay["const"] = constants(*(np.asarray(v) for v in (c, c_ctx, router_w, router_b, final_norm_g)))

    late = np.zeros((P, N_LATE), f32)
    late[:, LATE["before"]] = np.triu(np.ones((P, P)), 1) / D
    late[:, LATE["slots"]] = np.arange(NTOK)
    lay["late"] = late

    nc = bacc.Bacc("TRN2", target_bir_lowering=False, num_devices=1)
    arrays, args = {}, []
    for name, a in lay.items():
        arrays[f"in_{name}"] = np.ascontiguousarray(a)
        args.append(nc.dram_tensor(f"in_{name}", a.shape, F32, kind="ExternalInput").ap())
    args.append(nc.dram_tensor("outT", (D, LAT), F32, kind="ExternalOutput").ap())
    backbone(nc, *args)
    r = run_bass_kernel_spmd(nc, [arrays], core_ids=[0])
    return r.results[0]["outT"].T[None]
```
